# Optimizing a Trainium2 kernel written in Bass

```python
import jax
import jax.numpy as jnp
from jax import lax
import numpy as np

D_MODEL = 2048
BATCH = 1
SEQ = 256
DEPTH = 1
DEC_BATCH = 8
DEC_SEQ = 8
PAST_LEN = 2048
PAGE_SIZE = 128

C_CONV = 1024
CONV_W = 31
SW_GROUPS = 3
SW_WINDOWS = (128, 512, 2048)
SW_DILATIONS = (1, 4, 16)
SW_SPAN = 128
SW_HG = 4
SW_HD = 128
SW_OUT = SW_HG * SW_HD
SW_BLK = 128
N_MEM = 256
MEM_H = 4
MEM_HD = 256
MEM_W = MEM_H * MEM_HD
N_BRANCH = 3
IN_CONV = 2 * C_CONV
IN_SW = SW_GROUPS * 3 * SW_OUT
IN_MEMQ = MEM_W
IN_GATE = N_BRANCH * D_MODEL
IN_COLS = IN_CONV + IN_SW + IN_MEMQ + IN_GATE
PEER_HEADS = 8
PEER_NKEYS = 128
PEER_N = PEER_NKEYS * PEER_NKEYS
PEER_DKEY = 256
PEER_TOPK = 16
PEER_BLK = 128
EPS = 1e-6

kernel_name = 'hybrid_conv_dilated_mem_peer_step'

def rmsnorm(x, g):
    xf = x.astype(jnp.float32)
    y = xf * lax.rsqrt(jnp.mean(xf * xf, axis=-1, keepdims=True) + EPS)
    return (y * g.astype(jnp.float32)).astype(x.dtype)

def layernorm(x, g, b):
    xf = x.astype(jnp.float32)
    mu = jnp.mean(xf, axis=-1, keepdims=True)
    xc = xf - mu
    var = jnp.mean(xc * xc, axis=-1, keepdims=True)
    return (xc * lax.rsqrt(var + EPS) * g.astype(jnp.float32) + b.astype(jnp.float32)).astype(x.dtype)

def alibi_slopes():
    n = SW_GROUPS * SW_HG
    s = 2.0 ** (-8.0 * jnp.arange(1, n + 1, dtype=jnp.float32) / n)
    return s.reshape(SW_GROUPS, SW_HG)

def conv_branch(h_glu, prev, conv_w, conv_b, ln_g, ln_b, w_o):
    a, b = jnp.split(h_glu, 2, axis=-1)
    u = a * jax.nn.sigmoid(b)
    u_ext = jnp.concatenate([prev, u], axis=1)
    c = lax.conv_general_dilated(u_ext, conv_w[:, None, :].astype(u_ext.dtype), window_strides=(1,),
                                 padding='VALID', dimension_numbers=('NWC', 'WIO', 'NWC'),
                                 feature_group_count=C_CONV) + conv_b
    c = jax.nn.silu(layernorm(c, ln_g, ln_b))
    return c @ w_o, u_ext[:, -(CONV_W - 1):]

def dilated_band_attend(q, k, v, r, slopes):
    B, S, H, D = q.shape
    U = S // r
    nb = -(-U // SW_BLK)
    Up = nb * SW_BLK

    def classes(a):
        a = a.reshape(B, U, r, H, D).transpose(0, 2, 1, 3, 4)
        a = jnp.pad(a, ((0, 0), (0, 0), (0, Up - U), (0, 0), (0, 0)))
        return a.reshape(B, r, nb, SW_BLK, H, D)

    def band(a):
        prev = jnp.pad(a, ((0, 0), (0, 0), (1, 0), (0, 0), (0, 0), (0, 0)))[:, :, :nb]
        return jnp.concatenate([prev, a], axis=3)

    qb = classes(q)
    kw = band(classes(k))
    vw = band(classes(v)).astype(jnp.float32)
    s = jnp.einsum('brnihd,brnchd->brnhic', qb, kw).astype(jnp.float32)
    i = jnp.arange(SW_BLK)[:, None]
    c = jnp.arange(2 * SW_BLK)[None, :]
    j = SW_BLK + i - c
    u_key = (jnp.arange(nb)[:, None, None] - 1) * SW_BLK + c[None]
    valid = (j >= 0) & (j <= SW_SPAN) & (u_key >= 0)
    bias = -slopes[:, None, None] * (r * j).astype(jnp.float32)[None]
    s = jnp.where(valid[None, None, :, None], s + bias[None, None, None], -jnp.inf)
    m = jnp.max(s, axis=-1, keepdims=True)
    p = jnp.exp(s - m)
    l = jnp.sum(p, axis=-1, keepdims=True)
    o = jnp.einsum('brnhic,brnchd->brnhid', p, vw) / l
    lse = (m + jnp.log(l))[..., 0]
    o = o.transpose(0, 1, 2, 4, 3, 5).reshape(B, r, Up, H, D)[:, :, :U]
    o = o.transpose(0, 2, 1, 3, 4).reshape(B, S, H, D)
    lse = lse.transpose(0, 1, 2, 4, 3).reshape(B, r, Up, H)[:, :, :U]
    lse = lse.transpose(0, 2, 1, 3).reshape(B, S, H)
    return o, lse

def dilated_gather_attend(q, k_new, v_new, k_buf, v_buf, r, slopes):
    B, T, H, D = q.shape
    L = k_buf.shape[1]
    k_all = jnp.concatenate([k_buf, k_new], axis=1)
    v_all = jnp.concatenate([v_buf, v_new], axis=1)
    jj = jnp.arange(SW_SPAN + 1)
    idx = L + jnp.arange(T)[:, None] - r * jj[None, :]
    valid = idx >= 0
    idxc = jnp.maximum(idx, 0)
    kg = k_all[:, idxc]
    vg = v_all[:, idxc].astype(jnp.float32)
    s = jnp.einsum('bthd,btjhd->bhtj', q, kg).astype(jnp.float32)
    bias = -slopes[:, None, None] * (r * jj).astype(jnp.float32)[None, None, :]
    s = jnp.where(valid[None, None], s + bias[None], -jnp.inf)
    m = jnp.max(s, axis=-1, keepdims=True)
    p = jnp.exp(s - m)
    l = jnp.sum(p, axis=-1, keepdims=True)
    o = (jnp.einsum('bhtj,btjhd->bhtd', p, vg) / l).transpose(0, 2, 1, 3)
    lse = (m + jnp.log(l))[..., 0].transpose(0, 2, 1)
    return o, lse, k_all[:, T:], v_all[:, T:]

def combine_groups(outs, lses):
    wts = jax.nn.softmax(jnp.stack(lses, axis=0), axis=0)
    return jnp.einsum('gbth,gbthd->bthd', wts, jnp.stack(outs, axis=0))

def sw_prompt(q, k, v):
    T = q.shape[1]
    slopes = alibi_slopes()
    outs, lses, states = [], [], []
    for g in range(SW_GROUPS):
        o, lse = dilated_band_attend(q[:, :, g], k[:, :, g], v[:, :, g], SW_DILATIONS[g], slopes[g])
        outs.append(o)
        lses.append(lse)
        keep = min(SW_WINDOWS[g], T)
        states += [k[:, T - keep:, g], v[:, T - keep:, g]]
    return combine_groups(outs, lses), states

def sw_sample(q, k, v, bufs):
    slopes = alibi_slopes()
    outs, lses, states = [], [], []
    for g in range(SW_GROUPS):
        o, lse, kb, vb = dilated_gather_attend(q[:, :, g], k[:, :, g], v[:, :, g], bufs[2 * g], bufs[2 * g + 1],
                                               SW_DILATIONS[g], slopes[g])
        outs.append(o)
        lses.append(lse)
        states += [kb, vb]
    return combine_groups(outs, lses), states

def memory_kv(mem, mem_norm_g, w_k, w_v, k_g):
    B = mem.shape[0]
    mn = rmsnorm(mem, mem_norm_g)
    k = rmsnorm((mn @ w_k).reshape(B, N_MEM, MEM_H, MEM_HD), k_g)
    v = (mn @ w_v).reshape(B, N_MEM, MEM_H, MEM_HD)
    return k, v

def memory_attend(q, k, v):
    s = jnp.einsum('bthd,bshd->bhts', q, k).astype(jnp.float32)
    p = jax.nn.softmax(s, axis=-1).astype(v.dtype)
    return jnp.einsum('bhts,bshd->bthd', p, v)

def peer_ffn(xn, w_q, k1, k2, wu, wv):
    B, T, Dm = xn.shape
    n = B * T
    nb = -(-n // PEER_BLK)
    xt = jnp.pad(xn.reshape(n, Dm), ((0, nb * PEER_BLK - n), (0, 0))).reshape(nb, PEER_BLK, Dm)

    def block(xb):
        q = (xb @ w_q).reshape(PEER_BLK, PEER_HEADS, 2, PEER_DKEY // 2)
        s1 = jnp.einsum('thd,kd->thk', q[:, :, 0], k1).astype(jnp.float32)
        s2 = jnp.einsum('thd,kd->thk', q[:, :, 1], k2).astype(jnp.float32)
        v1, i1 = lax.top_k(s1, PEER_TOPK)
        v2, i2 = lax.top_k(s2, PEER_TOPK)
        cand = (v1[..., :, None] + v2[..., None, :]).reshape(PEER_BLK, PEER_HEADS, PEER_TOPK * PEER_TOPK)
        cidx = (i1[..., :, None] * PEER_NKEYS + i2[..., None, :]).reshape(PEER_BLK, PEER_HEADS, PEER_TOPK * PEER_TOPK)
        sv, si = lax.top_k(cand, PEER_TOPK)
        eidx = jnp.take_along_axis(cidx, si, axis=-1)
        gate = jax.nn.softmax(sv, axis=-1)
        act = jax.nn.gelu(jnp.einsum('td,thkd->thk', xb, wu[eidx]).astype(jnp.float32))
        coef = (gate * act).astype(xb.dtype)
        return jnp.einsum('thk,thkd->td', coef, wv[eidx])

    out = lax.map(block, xt).reshape(nb * PEER_BLK, Dm)[:n]
    return out.reshape(B, T, Dm)

def layer(x, conv_prev, sw_bufs, mem_k, mem_v, norm1_g, w_in, conv_w, conv_b, conv_ln_g, conv_ln_b, w_conv_o,
          sw_q_g, sw_k_g, w_sw_o, mem_q_g, w_mem_o, w_out, norm2_g, peer_w_q, peer_k1, peer_k2, peer_u, peer_v):
    B, T, _ = x.shape
    xn = rmsnorm(x, norm1_g)
    hcat = xn @ w_in
    h_conv, h_sw, h_mq, h_gate = jnp.split(hcat, [IN_CONV, IN_CONV + IN_SW, IN_CONV + IN_SW + IN_MEMQ], axis=-1)
    conv_out, conv_state = conv_branch(h_conv, conv_prev, conv_w, conv_b, conv_ln_g, conv_ln_b, w_conv_o)
    qkv = h_sw.reshape(B, T, SW_GROUPS, 3, SW_HG, SW_HD)
    q = rmsnorm(qkv[:, :, :, 0], sw_q_g[:, None, :]) * (SW_HD ** -0.5)
    k = rmsnorm(qkv[:, :, :, 1], sw_k_g[:, None, :])
    v = qkv[:, :, :, 2]
    if sw_bufs is None:
        sw_o, sw_states = sw_prompt(q, k, v)
    else:
        sw_o, sw_states = sw_sample(q, k, v, sw_bufs)
    sw_out = sw_o.astype(x.dtype).reshape(B, T, SW_OUT) @ w_sw_o
    qm = rmsnorm(h_mq.reshape(B, T, MEM_H, MEM_HD), mem_q_g) * (MEM_HD ** -0.5)
    mem_out = memory_attend(qm, mem_k, mem_v).reshape(B, T, MEM_W) @ w_mem_o
    gates = jax.nn.sigmoid(h_gate.reshape(B, T, N_BRANCH, D_MODEL))
    merged = gates[:, :, 0] * conv_out + gates[:, :, 1] * sw_out + gates[:, :, 2] * mem_out
    h = x + merged @ w_out
    y = h + peer_ffn(rmsnorm(h, norm2_g), peer_w_q, peer_k1, peer_k2, peer_u, peer_v)
    return y, conv_state, sw_states

def setup_inputs(seed: int = 0) -> dict:
    key = jax.random.key(seed)
    ks = iter(jax.random.split(key, 48))

    def nrm(shape, scale):
        return jax.random.normal(next(ks), shape, jnp.float32) * scale

    def gain(shape):
        return 1.0 + nrm(shape, 0.02)

    inp = {}
    inp['x_prompt'] = nrm((BATCH, SEQ, D_MODEL), 1.0)
    inp['x_sample'] = nrm((DEC_BATCH, DEC_SEQ, D_MODEL), 1.0)
    inp['mem_prompt'] = nrm((BATCH, N_MEM, D_MODEL), 1.0)
    inp['state_conv'] = nrm((DEPTH, DEC_BATCH, CONV_W - 1, C_CONV), 1.0)
    for g in range(SW_GROUPS):
        L = min(SW_WINDOWS[g], PAST_LEN)
        inp['state_sw%d_k' % g] = nrm((DEPTH, DEC_BATCH, L, SW_HG, SW_HD), 1.0)
        inp['state_sw%d_v' % g] = nrm((DEPTH, DEC_BATCH, L, SW_HG, SW_HD), 1.0)
    inp['cache_mem_k'] = nrm((DEPTH, DEC_BATCH, N_MEM, MEM_H, MEM_HD), 1.0)
    inp['cache_mem_v'] = nrm((DEPTH, DEC_BATCH, N_MEM, MEM_H, MEM_HD), 1.0)
    inp['norm1_g'] = gain((DEPTH, D_MODEL))
    inp['mem_norm_g'] = gain((DEPTH, D_MODEL))
    inp['w_in'] = nrm((DEPTH, D_MODEL, IN_COLS), D_MODEL ** -0.5)
    inp['conv_w'] = nrm((DEPTH, CONV_W, C_CONV), CONV_W ** -0.5)
    inp['conv_b'] = nrm((DEPTH, C_CONV), 0.01)
    inp['conv_ln_g'] = gain((DEPTH, C_CONV))
    inp['conv_ln_b'] = nrm((DEPTH, C_CONV), 0.01)
    inp['w_conv_o'] = nrm((DEPTH, C_CONV, D_MODEL), C_CONV ** -0.5)
    inp['sw_q_g'] = gain((DEPTH, SW_GROUPS, SW_HD))
    inp['sw_k_g'] = gain((DEPTH, SW_GROUPS, SW_HD))
    inp['w_sw_o'] = nrm((DEPTH, SW_OUT, D_MODEL), SW_OUT ** -0.5)
    inp['w_mem_k'] = nrm((DEPTH, D_MODEL, MEM_W), D_MODEL ** -0.5)
    inp['w_mem_v'] = nrm((DEPTH, D_MODEL, MEM_W), D_MODEL ** -0.5)
    inp['mem_q_g'] = gain((DEPTH, MEM_HD))
    inp['mem_k_g'] = gain((DEPTH, MEM_HD))
    inp['w_mem_o'] = nrm((DEPTH, MEM_W, D_MODEL), MEM_W ** -0.5)
    inp['w_out'] = nrm((DEPTH, D_MODEL, D_MODEL), D_MODEL ** -0.5)
    inp['norm2_g'] = gain((DEPTH, D_MODEL))
    inp['peer_w_q'] = nrm((DEPTH, D_MODEL, PEER_HEADS * PEER_DKEY), D_MODEL ** -0.5)
    inp['peer_k1'] = nrm((DEPTH, PEER_NKEYS, PEER_DKEY // 2), (PEER_DKEY // 2) ** -0.5)
    inp['peer_k2'] = nrm((DEPTH, PEER_NKEYS, PEER_DKEY // 2), (PEER_DKEY // 2) ** -0.5)
    inp['peer_u'] = nrm((DEPTH, PEER_N, D_MODEL), D_MODEL ** -0.5)
    inp['peer_v'] = nrm((DEPTH, PEER_N, D_MODEL), PEER_HEADS ** -0.5)
    return inp

def reference(x_prompt, x_sample, mem_prompt, state_conv, state_sw0_k, state_sw0_v, state_sw1_k, state_sw1_v,
              state_sw2_k, state_sw2_v, cache_mem_k, cache_mem_v, norm1_g, mem_norm_g, w_in, conv_w, conv_b,
              conv_ln_g, conv_ln_b, w_conv_o, sw_q_g, sw_k_g, w_sw_o, w_mem_k, w_mem_v, mem_q_g, mem_k_g, w_mem_o,
              w_out, norm2_g, peer_w_q, peer_k1, peer_k2, peer_u, peer_v):
    sw_bufs_all = (state_sw0_k, state_sw0_v, state_sw1_k, state_sw1_v, state_sw2_k, state_sw2_v)
    yp, ys = x_prompt, x_sample
    conv_p, conv_s, memk_p, memv_p = [], [], [], []
    sw_p = [[] for _ in range(2 * SW_GROUPS)]
    sw_s = [[] for _ in range(2 * SW_GROUPS)]
    for l in range(DEPTH):
        lw = (norm1_g[l], w_in[l], conv_w[l], conv_b[l], conv_ln_g[l], conv_ln_b[l], w_conv_o[l], sw_q_g[l],
              sw_k_g[l], w_sw_o[l], mem_q_g[l], w_mem_o[l], w_out[l], norm2_g[l], peer_w_q[l], peer_k1[l],
              peer_k2[l], peer_u[l], peer_v[l])
        mk, mv = memory_kv(mem_prompt, mem_norm_g[l], w_mem_k[l], w_mem_v[l], mem_k_g[l])
        zeros_prev = jnp.zeros((yp.shape[0], CONV_W - 1, C_CONV), yp.dtype)
        yp, cp, sp = layer(yp, zeros_prev, None, mk, mv, *lw)
        ys, cs, ss = layer(ys, state_conv[l], [b[l] for b in sw_bufs_all], cache_mem_k[l], cache_mem_v[l], *lw)
        conv_p.append(cp)
        conv_s.append(cs)
        memk_p.append(mk)
        memv_p.append(mv)
        for i in range(2 * SW_GROUPS):
            sw_p[i].append(sp[i])
            sw_s[i].append(ss[i])
    swp = [jnp.stack(a, axis=0) for a in sw_p]
    sws = [jnp.stack(a, axis=0) for a in sw_s]
    return (yp, ys, jnp.stack(conv_p, axis=0), jnp.stack(conv_s, axis=0),
            swp[0], swp[1], swp[2], swp[3], swp[4], swp[5],
            sws[0], sws[1], sws[2], sws[3], sws[4], sws[5],
            jnp.stack(memk_p, axis=0), jnp.stack(memv_p, axis=0))


_drawn_inputs = setup_inputs


def setup_inputs(seed=0):
    import zlib

    import numpy as np

    out = dict(_drawn_inputs(seed))
    spreads = {}
    factors = {'norm1_g': 2.667,
     'mem_norm_g': 2.765,
     'conv_b': 3.746,
     'conv_ln_g': 11.101,
     'conv_ln_b': 22.542,
     'sw_q_g': 5.835,
     'sw_k_g': 2.773,
     'mem_q_g': 8.0,
     'mem_k_g': 3.048,
     'norm2_g': 12.312}
    for name, (base, spread) in spreads.items():
        noise = np.random.default_rng([zlib.crc32(name.encode()), seed]).standard_normal(out[name].shape)
        drawn = base * np.exp(spread * noise) if base else spread * noise
        out[name] = jnp.asarray(drawn.astype(out[name].dtype))
    for name, factor in factors.items():
        out[name] = (out[name] * factor).astype(out[name].dtype)
    return out
```

```python
from contextlib import ExitStack

import concourse.bass as bass
from concourse import mybir

F32 = mybir.dt.float32
F32R = mybir.dt.float32r
U32 = mybir.dt.uint32
ALU = mybir.AluOpType
ACT = mybir.ActivationFunctionType
AX = mybir.AxisListType

P = 128
D = 2048
KT = D // P
NP, NB, NS = 256, 8, 8
NT = NP + NB * NS
CC, CW = 1024, 31
CT = CC // P
G, HG = 3, 4
WINDOWS, DILATIONS = (128, 512, 2048), (1, 4, 16)
UNITS = sum(min(r, NS) for r in DILATIONS)
NM, MH, MD = 256, 4, 256
PH, PK, TOPK = 8, 128, 16
EPS = 1e-6
BLK = 1024

MEMK_BLOCKS, MEMV_BLOCKS, PROJ_BLOCKS, GATE_BLOCKS = 16, 16, 120, 96
OPROJ_BLOCKS, OUT_BLOCKS, WQ_BLOCKS, U_BLOCKS, V_BLOCKS = 40, 32, 32, 256, 256
MEMK0 = 0
MEMV0 = MEMK0 + MEMK_BLOCKS
PROJ0 = MEMV0 + MEMV_BLOCKS
GATE0 = PROJ0 + PROJ_BLOCKS
OPROJ0 = GATE0 + GATE_BLOCKS
OUT0 = OPROJ0 + OPROJ_BLOCKS
WQ0 = OUT0 + OUT_BLOCKS
U0 = WQ0 + WQ_BLOCKS
V0 = U0 + U_BLOCKS
END = V0 + V_BLOCKS
MEMK_T, MEMV_T, PROJ_T, GATE_T = 0, 8, 12, 72
OUT_T, WQ_T, U_T, V_T = 120, 136, 152, 280

SELECT_TILES = 5
SPREAD_U = SELECT_TILES * PH
LAST_U = SPREAD_U + NT // 4
SAMPLE_COLS = G * P + G * NS
NEG = -1.0e30


class Place:

    def __init__(self, const, *terms):
        self.const, self.terms = const, terms

    def __add__(self, k):
        return Place(self.const + k, *self.terms)

    def over(self, d):
        return Place(self.const // d, *[(per // d, reg) for per, reg in self.terms])

    def value(self, scale=1, plus=0):
        total = self.const * scale + plus
        for per, reg in self.terms:
            total = reg * (per * scale) + total
        return total


def slopes():
    n = G * HG
    return [2.0 ** (-8.0 * (i + 1) / n) for i in range(n)]


def build(nc, a, o):
    ctx = ExitStack()
    with ctx:
        def sb(name, shape, dt=F32, scope=ctx):
            return scope.enter_context(nc.sbuf_tensor(name, shape, dt))

        def sem(name):
            return ctx.enter_context(nc.semaphore(name))

        def scratch(name, shape):
            return nc.dram_tensor(name, shape, F32, kind="Internal").ap()

        raw = sb("raw", [P, 4, BLK])
        w_hi = sb("w_hi", [P, 4, BLK], F32R)
        w_lo = sb("w_lo", [P, 4, BLK], F32R)
        xs_hi = sb("xs_hi", [P, KT, NT], F32R)
        xs_lo = sb("xs_lo", [P, KT, NT], F32R)
        ident = sb("ident", [P, P])
        iota = sb("iota", [P, P])
        iota16 = sb("iota16", [P, TOPK])
        slope = sb("slope", [P, G * HG])
        ones = sb("ones", [P, P])
        prm = sb("prm", [P, a["params"].shape[1]])
        at = 0

        def param(n):
            nonlocal at
            at += n
            return prm[:, at - n:at]

        g1, gm, g2 = param(KT), param(KT), param(KT)
        cw, cb, lng, lnb = param(CT * CW), param(CT), param(CT), param(CT)
        qg, kg, mqg, mkg = param(G), param(G), param(2), param(2)
        k1T, k2T = param(PK), param(PK)

        low, high = ExitStack(), ExitStack()
        x_raw = sb("x_raw", [P, KT, NT], scope=low)
        m_raw = sb("m_raw", [P, KT, NM], scope=low)
        sq4 = sb("sq4", [P, 4, NT], scope=low)
        rms_x = sb("rms_x", [P, 2, NT], scope=low)
        low.close()
        low = ExitStack()
        hb = sb("hb", [P, 44, NT], scope=low)
        mk = sb("mk", [P, 2 * MH, NM], scope=high)
        mv = sb("mv", [P, 2, MH * MD], scope=high)
        PW, SWD = NP + CW - 1, NS + CW - 1
        ue = sb("ue", [P, CT, PW + NB * SWD], scope=high)
        cc = sb("cc", [P, CT, NT], scope=high)
        sig = sb("sig", [P, NT], scope=high)
        rms_c = sb("rms_c", [P, 2, NT], scope=high)
        gate_st = sb("gate_st", [P, 4, NT], scope=high)
        high.close()
        high = ExitStack()
        vnp = sb("vnp", [P, 2, G * HG, P], scope=high)
        nnew = sb("nnew", [NB * NS, 2, G * HG * P], scope=high)
        sS = sb("sS", [P, G * P + G * NP], scope=high)
        pT = sb("pT", [P, G * P + G * NP], scope=high)
        dpr = sb("dpr", [P, 2, G, NP], scope=high)
        stat = sb("stat", [P, 8], scope=high)
        ex = ExitStack()
        q_st = sb("q_st", [P, G, NP], scope=ex)
        v_st = sb("v_st", [P, 2, G, P], scope=ex)
        qk_sq = sb("qk_sq", [P, HG, NT], scope=ex)
        qk_r = sb("qk_r", [P, HG, NT], scope=ex)
        ex.close()
        ex = ExitStack()
        km = sb("km", [P, 2, 2 * MH * NM], scope=ex)
        mq_st = sb("mq_st", [P, 2, NP], scope=ex)
        mv_st = sb("mv_st", [P, 2, MD], scope=ex)
        zm = sb("zm", [P, 2, MH, 32], scope=ex)
        ex.close()
        high.close()
        high = ExitStack()
        kv = sb("kv", [P, 4, HG * P], scope=high)
        vnew = sb("vnew", [NS, G * HG * P], scope=high)
        z = sb("z", [P, UNITS + 2, HG, 32], scope=high)
        zn = sb("zn", [NS, G, HG, 32], scope=high)
        kn = sb("kn", [P, G * HG, NS], scope=high)
        dsm = sb("dsm", [P, SAMPLE_COLS], scope=high)
        sT = sb("sT", [P, SAMPLE_COLS], scope=high)
        pTs = sb("pTs", [P, G * P], scope=high)
        pTn = sb("pTn", [NS, G * P], scope=high)
        osb = sb("osb", [P, MD], scope=high)
        stat2 = sb("stat2", [P, 8], scope=high)
        high.close()
        high = ExitStack()
        osw_hi = sb("osw_hi", [P, HG, NT], F32R, scope=high)
        osw_lo = sb("osw_lo", [P, HG, NT], F32R, scope=high)
        gl = sb("gl", [P, 2, 3, NT], scope=high)
        mt = sb("mt", [P, 4, NT], scope=high)
        high.close()
        low.close()
        low = ExitStack()
        xs2_hi = sb("xs2_hi", [P, KT, NT], F32R, scope=low)
        xs2_lo = sb("xs2_lo", [P, KT, NT], F32R, scope=low)
        acc = sb("acc", [P, KT, NT], scope=low)
        gelu_st = sb("gelu_st", [P, 2, NT], scope=low)
        T = sb("T", [P, 3, NT], scope=low)
        ph = ExitStack()
        qT = sb("qT", [P, 2 * PH, NT], scope=ph)
        ex = ExitStack()
        sqh = sb("sqh", [P, 4, NT], scope=ex)
        rms_h = sb("rms_h", [P, 2, NT], scope=ex)
        ex.close()
        pq_st = sb("pq_st", [P, 2, NT], scope=ph)
        tS = sb("tS", [P, 6 * PK], scope=ph)
        tW = sb("tW", [P, 6 * PK], scope=ph)
        eq = sb("eq", [P, 3, TOPK, TOPK], scope=ph)
        tv = sb("tv", [P, 6, TOPK], scope=ph)
        tiu = sb("tiu", [P, 6, TOPK], U32, scope=ph)
        tif = sb("tif", [P, 6, TOPK], scope=ph)
        cv = sb("cv", [P, 3, TOPK], scope=ph)
        ci = sb("ci", [P, 3, TOPK], U32, scope=ph)
        cab = sb("cab", [P, 2, 3, TOPK], U32, scope=ph)
        cabf = sb("cabf", [P, 2, 3, TOPK], scope=ph)
        ce = sb("ce", [P, 3, TOPK], scope=ph)
        tz = sb("tz", [P, 12], scope=ph)
        R = sb("R", [P, 3, 3, PH, TOPK], scope=ph)
        ph.close()
        ph = ExitStack()
        hot = sb("hot", [P, 2, 4, 2, PK], scope=ph)
        gd = sb("gd", [P, 2, PK, 32], scope=ph)
        ph.close()
        ph = ExitStack()
        actc = sb("actc", [P, 2, 4, NT], scope=ph)
        gc = sb("gc", [P, 2, NT // 32, 4, 32], scope=ph)
        cf = sb("cf", [P, 2, 2, NT], scope=ph)
        ph.close()
        low.close()

        ps = ctx.enter_context(nc.psum_tensor("ps", [P, 8, 512], F32))

        gates_d = scratch("gates_d", [3 * KT, P, NT])
        new_d = scratch("new_d", [2, NB * NS, G * HG * P])
        act_d = scratch("act_d", [P, P, NT])
        gd_d = scratch("gd_d", [NT // 32, P, PK * 32])

        m_loaded, x_loaded, const_loaded = sem("m_loaded"), sem("x_loaded"), sem("const_loaded")
        raw_loaded = [sem(f"raw_loaded{i}") for i in range(4)]
        hi_done, lo_done, w_released = sem("hi_done"), sem("lo_done"), sem("w_released")
        bank_free = sem("bank_free")
        sq_done, sq_summed, rooted, normed = sem("sq_done"), sem("sq_summed"), sem("rooted"), sem("normed")
        xs_hi_done, xs_lo_done = sem("xs_hi_done"), sem("xs_lo_done")
        dve_set, mv_taken = sem("dve_set"), sem("mv_taken")
        state_copied, conv_prev_loaded = sem("state_copied"), sem("conv_prev_loaded")
        sig_done = sem("sig_done")
        gates_stored = [sem(f"gates_stored{i}") for i in range(4)]
        conv_done, ln_summed, ln_centered = sem("conv_done"), sem("ln_summed"), sem("ln_centered")
        ln_squared, ln_rooted, ln_scaled, silu_done = sem("ln_squared"), sem("ln_rooted"), sem("ln_scaled"), sem("silu_done")
        mk_ready = sem("mk_ready")
        conv_stored, mem_stored, kp_stored, vp_stored = (
            sem("conv_stored"), sem("mem_stored"), sem("kp_stored"), sem("vp_stored"))
        vt_turned, vt_copied, new_stored, tails_copied = (
            sem("vt_turned"), sem("vt_copied"), sem("new_stored"), sem("tails_copied"))
        dist_p_loaded, dist_s_loaded = sem("dist_p_loaded"), sem("dist_s_loaded")
        a_staged, a_scored, a_biased, a_exped = sem("a_staged"), sem("a_scored"), sem("a_biased"), sem("a_exped")
        a_probs, a_turned, a_copied, a_mixed, a_kept = (
            sem("a_probs"), sem("a_turned"), sem("a_copied"), sem("a_mixed"), sem("a_kept"))
        m_staged, m_scored, m_maxed, m_exped, m_probs = (
            sem("m_staged"), sem("m_scored"), sem("m_maxed"), sem("m_exped"), sem("m_probs"))
        m_turned, m_copied, m_mixed, m_kept = sem("m_turned"), sem("m_copied"), sem("m_mixed"), sem("m_kept")
        km_loaded = [sem("km_loaded0"), sem("km_loaded1")]
        zm_set, zm_used = sem("zm_set"), sem("zm_used")
        n_maxed, n_exped, n_probs, n_turned = sem("n_maxed"), sem("n_exped"), sem("n_probs"), sem("n_turned")
        n_copied, n_out, n_back, n_kept = sem("n_copied"), sem("n_out"), sem("n_back"), sem("n_kept")
        kv_loaded = [sem(f"kv_loaded{i}") for i in range(4)]
        kv_used, z_set, z_used, vnew_loaded = sem("kv_used"), sem("z_set"), sem("z_used"), sem("vnew_loaded")
        s_maxed, s_exped, s_probs, s_turned = sem("s_maxed"), sem("s_exped"), sem("s_probs"), sem("s_turned")
        s_copied, s_out, s_back, s_kept = sem("s_copied"), sem("s_out"), sem("s_back"), sem("s_kept")
        osw_hi_done, osw_lo_done = sem("osw_hi_done"), sem("osw_lo_done")
        gl_loaded, o_taken = [sem("gl_loaded0"), sem("gl_loaded1")], sem("o_taken")
        merged, merged_hi, merged_lo, acc_loaded = sem("merged"), sem("merged_hi"), sem("merged_lo"), sem("acc_loaded")
        act_stored = [sem("act_stored0"), sem("act_stored1")]
        t_staged, t_scored, t_picked, t_exped, r_done = (
            sem("t_staged"), sem("t_scored"), sem("t_picked"), sem("t_exped"), sem("r_done"))
        r_turned, t_set, hot_set, hot_used, g_spread = (
            sem("r_turned"), sem("t_set"), sem("hot_set"), sem("hot_used"), sem("g_spread"))
        gd_stored = [sem("gd_stored0"), sem("gd_stored1")]
        chunk_loaded = [sem("chunk_loaded0"), sem("chunk_loaded1")]
        c_made, c_hi, c_lo = sem("c_made"), sem("c_hi"), sem("c_lo")
        y_stored = sem("y_stored")

        def taken(t):
            return t + 3

        def tile_view(t, i, lo=0, n=NT):
            return t[:, bass.ds(i, 1), lo:lo + n].rearrange("p o n -> p (o n)")

        def strided(view, offset, dims):
            return bass.AP(view.tensor, view.offset + offset, [list(view.ap[0])] + dims)

        DIAG = 32 + NS
        ZU = HG * 32

        def z_views(zt, src_of):
            zz = zt[:, :, :, :]
            return [
                (strided(zz, 0, [[DIAG, HG], [1, NS]]), src_of(0)),
                (strided(zz, ZU, [[ZU + 1, 4], [DIAG, HG], [4, 2]]),
                 src_of(1).rearrange("p h (i c) -> p c h i", c=4)),
                (strided(zz, 5 * ZU, [[ZU + 1, NS], [DIAG, HG]]), src_of(2).rearrange("p h t -> p t h")),
            ]

        block = ctx.enter_context(nc.Block())

        @block.sync
        def _(sp):
            def load(src, i, n):
                if n.const >= 4 or n.terms:
                    sp.wait_ge(lo_done, n.value(plus=-3))
                sp.dma_start(raw[:, n.const % 4, :],
                             src[bass.ds(i, 1)].rearrange("o p n -> (o p) n")).then_inc(raw_loaded[n.const % 4], 16)

            def rest_of_stage(src, base, blocks):
                with sp.Fori(1, blocks // 4) as i:
                    for r in range(4):
                        load(src, i * 4 + r, Place(base + r, (4, i)))

            def first_of_stage(src, base):
                for r in range(4):
                    load(src, r, Place(base + r))

            sp.dma_start(m_raw[:], a["memT"]).then_inc(m_loaded, 16)
            sp.dma_start(x_raw[:], a["xT"]).then_inc(x_loaded, 16)
            for name, base, blocks in (("w_memk", MEMK0, MEMK_BLOCKS), ("w_memv", MEMV0, MEMV_BLOCKS),
                                       ("w_proj", PROJ0, PROJ_BLOCKS), ("w_gate", GATE0, GATE_BLOCKS)):
                first_of_stage(a[name], base)
                rest_of_stage(a[name], base, blocks)
            first_of_stage(a["w_oproj"], OPROJ0)

            sp.wait_ge(mem_stored, 16 * 2)
            sp.wait_ge(a_kept, HG)
            sp.dma_start(km[:, 0, :], o["memk"].rearrange("p t n -> p (t n)")).then_inc(km_loaded[0], 16)
            sp.dma_start(km[:, 1, :].rearrange("p (s n) -> p s n", s=2),
                         o["memv"].rearrange("s p n -> p s n")).then_inc(km_loaded[1], 16)
            sp.wait_ge(m_kept, MH)
            with sp.Fori(0, 2) as i:
                for part in range(2):
                    for bq in range(4):
                        sp.wait_ge(zm_used, i * 8 + (part * 4 + bq + 1))
                        sp.dma_start(km[:, bq % 2, :], (a["memv_c"] if part else a["memk_c"])[
                            bass.ds(i * 4 + bq, 1)].rearrange("o p n -> (o p) n")).then_inc(km_loaded[bq % 2], 16)
            sp.wait_ge(n_kept, 2)
            sp.wait_ge(new_stored, 16 * 2)
            sp.wait_ge(vp_stored, 16)
            with sp.Fori(0, 2) as i:
                for part, name in enumerate(("k_units", "v_units")):
                    units = a[name].rearrange("b u p n -> (b u) p n")
                    with sp.Fori(0, UNITS) as j:
                        for r in range(4):
                            sp.wait_ge(kv_used, i * (8 * UNITS) + j * 4 + (part * 4 * UNITS + r + 1))
                            sp.dma_start(kv[:, r, :], units[bass.ds(i * (4 * UNITS) + j * 4 + r, 1)].rearrange(
                                "o p n -> (o p) n")).then_inc(kv_loaded[r], 16)
            rest_of_stage(a["w_oproj"], OPROJ0, OPROJ_BLOCKS)
            for name, base, blocks in (("w_out", OUT0, OUT_BLOCKS), ("w_q", WQ0, WQ_BLOCKS),
                                       ("w_u", U0, U_BLOCKS), ("w_v", V0, V_BLOCKS)):
                first_of_stage(a[name], base)
                rest_of_stage(a[name], base, blocks)
            sp.wait_ge(bank_free, taken(V_T + V_BLOCKS // 2 - 1))
            sp.dma_start(o["y"], acc[:]).then_inc(y_stored, 16)
            for s, n in ((y_stored, 1), (conv_stored, 1 + CT), (mem_stored, 2), (kp_stored, G), (vp_stored, 1),
                         (state_copied, 2 * G * NB), (tails_copied, 2 * G)):
                sp.wait_ge(s, 16 * n)

        @block.gpsimd
        def _(pool):
            for dst, name in ((ident, "ident"), (iota, "iota"), (iota16, "iota16"), (slope, "slope"), (prm, "params")):
                pool.dma_start(dst[:], a[name]).then_inc(const_loaded, 16)
            for ct in range(CT):
                pool.dma_start(ue[:, ct, PW:].rearrange("p (b w) -> p b w", b=NB)[:, :, 0:CW - 1],
                               a["conv_state"][:, ct]).then_inc(conv_prev_loaded, 16)

            def keep_state(b, name):
                for g in range(G):
                    keep = (WINDOWS[g] - NS) * HG * P
                    src = a[f"sw{g}_{name}"][bass.ds(b, 1), NS * HG * P:].rearrange("o (c n) -> (o c) n", c=16)
                    dst = o[f"sw{g}_{name}"][bass.ds(b, 1), 0:keep].rearrange("o (c n) -> (o c) n", c=16)
                    pool.dma_start(dst, src).then_inc(state_copied, 16)

            with pool.Fori(0, NB) as b:
                pool.wait_ge(bank_free, b * 7 + taken(PROJ_T))
                keep_state(b + 0, "k")
            with pool.Fori(0, NB) as b:
                pool.wait_ge(bank_free, b * 6 + taken(GATE_T))
                keep_state(b + 0, "v")
            pool.wait_ge(bank_free, taken(PROJ_T + 2 * CT - 1))
            pool.dma_start(o["convp"], ue[:, :, NP:PW]).then_inc(conv_stored, 16)
            for ct in range(CT):
                pool.dma_start(o["convs"][:, ct], ue[:, ct, PW:].rearrange("p (b w) -> p b w", b=NB)[:, :, NS:SWD]
                               ).then_inc(conv_stored, 16)
            pool.wait_ge(mk_ready, 1)
            pool.dma_start(o["memk"], mk[:]).then_inc(mem_stored, 16)
            pool.dma_start(o["memv"].rearrange("s p n -> p s n"), mv[:]).then_inc(mem_stored, 16)
            pool.wait_ge(xs_lo_done, 3)
            pool.wait_ge(conv_stored, 16 * (1 + CT))
            pool.wait_ge(mem_stored, 16 * 2)
            pool.dma_start(dpr[:], a["dist_p"]).then_inc(dist_p_loaded, 16)
            pool.wait_ge(normed, 3 + 2 * G)
            for g in range(G):
                pool.dma_start(o["kp"][:, g * HG:(g + 1) * HG, :], hb[:, g * 12 + 4:g * 12 + 8, 0:NP]).then_inc(
                    kp_stored, 16)
            pool.wait_ge(vt_copied, 4 * G)
            pool.dma_start(o["vp"], vnp[:]).then_inc(vp_stored, 16)
            for part in range(2):
                pool.dma_start(new_d[part], nnew[:, part, :]).then_inc(new_stored, 16)
            pool.wait_ge(new_stored, 16 * 2)
            for g in range(G):
                for part, name in enumerate("kv"):
                    src = new_d[part].rearrange("(b t) c -> b t c", b=NB)[:, :, g * HG * P:(g + 1) * HG * P]
                    dst = o[f"sw{g}_{name}"].rearrange("b (l c) -> b l c", c=HG * P)[:, WINDOWS[g] - NS:, :]
                    pool.dma_start(dst, src).then_inc(tails_copied, 16)
            pool.wait_ge(n_kept, 2)
            pool.wait_ge(vp_stored, 16)
            pool.dma_start(dsm[:], a["dist_s"]).then_inc(dist_s_loaded, 16)
            pool.wait_ge(new_stored, 16 * 2)
            with pool.Fori(0, 2) as i:
                for bq in range(4):
                    pool.wait_ge(z_used, i * 8 + (5 + bq))
                    pool.dma_start(vnew[:], new_d[1, bass.ds(i * 32 + NS * bq, NS), :]).then_inc(vnew_loaded, 16)
            pool.wait_ge(s_kept, 2)
            for s in gates_stored:
                pool.wait_ge(s, 16 * (3 * KT // 4))
            by_tile = gates_d.rearrange("(b m) p n -> m p b n", b=3)
            with pool.Fori(0, KT // 2) as i:
                for r in range(2):
                    pool.wait_ge(o_taken, i * 2 + (r + 1))
                    pool.dma_start(gl[:, r], by_tile[bass.ds(i * 2 + r, 1)].rearrange("o p b n -> (o p) b n")
                                   ).then_inc(gl_loaded[r], 16)
            pool.wait_ge(w_released, OUT0)
            pool.wait_ge(o_taken, KT + 2)
            pool.dma_start(acc[:], a["xT"]).then_inc(acc_loaded, 16)

            def store_gelu(m, r, gelu_taken):
                pool.wait_ge(bank_free, gelu_taken)
                pool.dma_start(act_d[bass.ds(m, 1)].rearrange("o p n -> (o p) n"),
                               gelu_st[:, r, :]).then_inc(act_stored[r], 16)

            def load_chunk(q, c):
                pool.dma_start(actc[:, c], act_d[bass.ds(q * 4, 4)].rearrange("i p n -> p i n")
                               ).then_inc(chunk_loaded[c], 16)
                pool.dma_start(gc[:, c].rearrange("p b i t -> p b (i t)"),
                               gd_d[:, :, bass.ds(q * 128, 128)].rearrange("b p n -> p b n")
                               ).then_inc(chunk_loaded[c], 16)

            with pool.Fori(0, PH // 2) as h2:
                for j in range(2 * SELECT_TILES):
                    store_gelu(h2 * 10 + j, j % 2, h2 * 10 + taken(U_T + j))
            with pool.Fori(0, NT // 64) as tb:
                for s in range(2):
                    for m in range(8):
                        k = SPREAD_U + s * 8 + m
                        store_gelu(tb * 16 + k, m % 2, tb * 16 + taken(U_T + k))
                    pool.wait_ge(g_spread, tb * 16 + (2 + (s + 1) * 8))
                    pool.dma_start(gd_d[bass.ds(tb * 2 + s, 1)].rearrange("o p n -> (o p) n"),
                                   gd[:, s].rearrange("p i t -> p (i t)")).then_inc(gd_stored[s], 16)
            for s in range(2):
                pool.wait_ge(gd_stored[s], 16 * (NT // 64))
            for s in act_stored:
                pool.wait_ge(s, 16 * (LAST_U // 2))
            load_chunk(0, 0)
            load_chunk(1, 1)
            for q in range(4):
                for r in range(2):
                    k = LAST_U + 2 * q + r
                    store_gelu(k, r, taken(U_T + k))
                pool.wait_ge(c_made, 2 * q + 2)
                load_chunk(q + 2, q % 2)
            for s in act_stored:
                pool.wait_ge(s, 16 * (P // 2))
            with pool.Fori(3, 16) as i:
                for c in range(2):
                    pool.wait_ge(c_made, i * 4 + (2 * c - 2))
                    load_chunk(i * 2 + c, c)

        @block.scalar
        def _(act):
            A = act.activation

            def split_hi(n):
                s = n.const % 4
                act.wait_ge(raw_loaded[s], n.over(4).value(16, 16))
                if n.const >= 4 or n.terms:
                    act.wait_ge(w_released, n.value(plus=-3))
                A(w_hi[:, s, :], raw[:, s, :], ACT.Copy).then_inc(hi_done, 1)

            def width_norm(src, cols, k, sq, root, bank):
                for c in range(4):
                    if c:
                        act.wait_ge(sq_summed, 4 * k + c)
                    A(sq[:, :, 0:cols], src[:, 4 * c:4 * c + 4, :], ACT.Square).then_inc(sq_done, 1)
                act.wait_ge(sq_summed, 4 * k + 4)
                A(root[:, 0, 0:cols], ps[:, bank, 0:cols], ACT.Sqrt, bias=EPS, scale=1.0 / D).then_inc(rooted, 1)

            act.sem_inc(g_spread, 2)
            act.wait_ge(m_loaded, 16)
            width_norm(m_raw, NM, 0, sq4, rms_x, 2)
            act.wait_ge(normed, 1)
            A(xs_hi[:, :, 0:NM], m_raw[:], ACT.Copy).then_inc(xs_hi_done, 1)
            for n in range(4):
                split_hi(Place(n))
            act.wait_ge(x_loaded, 16)
            width_norm(x_raw, NT, 1, sq4, rms_x, 3)
            with act.Fori(0, (MEMK_BLOCKS + MEMV_BLOCKS) // 4) as i:
                for r in range(4):
                    split_hi(Place(4 + r, (4, i)))
            act.wait_ge(w_released, PROJ0)
            act.wait_ge(normed, 2)
            A(xs_hi[:], x_raw[:], ACT.Copy).then_inc(xs_hi_done, 1)
            with act.Fori(0, CT // 2) as i:
                for u in range(2):
                    n = Place(PROJ0 + 4 * u, (8, i))
                    for r in range(4):
                        split_hi(n + (r + 4))
                    act.wait_ge(bank_free, i * 4 + taken(PROJ_T + 2 * u - 1))
                    A(sig[:], ps[:, 2 * u + 1, 0:NT], ACT.Sigmoid).then_inc(sig_done, 1)
            with act.Fori(0, 22) as i:
                n = Place(PROJ0 + 4 * CT, (4, i))
                for j in range(2):
                    split_hi(n + (2 * j + 4))
                    split_hi(n + (2 * j + 5))
                    act.copy(tile_view(hb, i * 2 + j), ps[:, j, 0:NT]).then_inc(bank_free, 1)

            def store_gate(i, j):
                if i is None:
                    act.wait_ge(bank_free, taken(GATE_T + j))
                    dst = gates_d[j]
                else:
                    act.wait_ge(bank_free, i * 4 + taken(GATE_T + j))
                    dst = gates_d[bass.ds(i * 4 + j, 1)].rearrange("o p n -> (o p) n")
                act.dma_start(dst, gate_st[:, j, :]).then_inc(gates_stored[j], 16)

            def gates(n, i):
                for j in range(4):
                    split_hi(n + (2 * j + 4))
                    split_hi(n + (2 * j + 5))
                    if i is not None:
                        act.wait_ge(gates_stored[j], i * 16)
                    A(gate_st[:, j, :], ps[:, j % 2, 0:NT], ACT.Sigmoid).then_inc(bank_free, 1)
                    store_gate(i, j)

            gates(Place(GATE0), None)
            with act.Fori(1, 3 * KT // 4) as i:
                gates(Place(GATE0, (8, i)), i)

            for s in gates_stored:
                act.wait_ge(s, 16 * (3 * KT // 4))
            act.wait_ge(ln_centered, 1)
            for c in range(2):
                if c:
                    act.wait_ge(ln_summed, 2)
                A(gate_st[:], cc[:, 4 * c:4 * c + 4, :], ACT.Square).then_inc(ln_squared, 1)
            act.wait_ge(ln_summed, 3)
            A(rms_c[:, 0, :], ps[:, 3, 0:NT], ACT.Sqrt, bias=EPS, scale=1.0 / CC).then_inc(ln_rooted, 1)
            for c in range(2):
                act.wait_ge(ln_summed, 3 + c)
                A(gate_st[:, :, 0:NM], mk[:, 4 * c:4 * c + 4, :], ACT.Square).then_inc(ln_squared, 1)
            act.wait_ge(ln_summed, 5)
            A(gate_st[:, :, 0:NM].rearrange("p (b h) n -> p b h n", b=2),
              ps[:, 4:6, :].rearrange("p b (h n) -> p b h n", h=2), ACT.Sqrt, bias=EPS, scale=1.0 / MD
              ).then_inc(ln_rooted, 1)
            act.wait_ge(ln_scaled, 1)
            for ct in range(CT):
                A(cc[:, ct, :], cc[:, ct, :], ACT.Silu, bias=lnb[:, ct:ct + 1], scale=lng[:, ct:ct + 1])
            act.drain()
            act.wait_ge(w_released, OPROJ0)
            A(xs_hi[:, 0:CT, :], cc[:], ACT.Copy).then_inc(xs_hi_done, 1)

            act.wait_ge(xs_lo_done, 3)
            act.wait_ge(mem_stored, 32)
            act.wait_ge(conv_stored, 16 * (1 + CT))
            for k in range(2 * G + 2):
                first = (k // 2) * 12 + (k % 2) * HG if k < 2 * G else 36 + (k - 2 * G) * HG
                if k:
                    act.wait_ge(normed, 3 + k - 1)
                A(qk_sq[:], hb[:, first:first + HG, :], ACT.Square).then_inc(sq_done, 1)
                act.wait_ge(sq_summed, 8 + k + 1)
                if k >= 2 * G:
                    A(qk_r[:, 0:2, :], ps[:, 2:4, 0:NT], ACT.Sqrt, bias=MD * EPS).then_inc(rooted, 1)
                elif k % 2:
                    A(qk_r[:], ps[:, 2:6, 0:NT], ACT.Sqrt, bias=EPS, scale=1.0 / P).then_inc(rooted, 1)
                else:
                    A(qk_r[:], ps[:, 2:6, 0:NT], ACT.Sqrt, bias=P * EPS).then_inc(rooted, 1)

            S0, S1 = slice(0, G * P), slice(G * P, G * (P + NP))
            with act.Fori(0, HG) as h:
                act.wait_ge(a_biased, h + 1)
                for qb, cols in enumerate((S0, S1)):
                    e = A(sS[:, cols], sS[:, cols], ACT.Exp, bias=stat[:, qb:qb + 1], accum_out=stat[:, 2 + qb:3 + qb])
                e.then_inc(a_exped, 1)
                act.wait_ge(a_turned, h + 1)
                act.copy(pT[:, 0:3 * P], ps[:, 5, 0:3 * P])
                act.copy(pT[:, 3 * P:9 * P], ps[:, 6:8, 0:3 * P]).then_inc(a_copied, 1)

            with act.Fori(0, MH) as h:
                act.wait_ge(m_maxed, h + 1)
                for qb in range(2):
                    e = A(sS[:, qb * NM:(qb + 1) * NM], ps[:, 2, qb * NM:(qb + 1) * NM], ACT.Exp,
                          bias=stat[:, qb:qb + 1], accum_out=stat[:, 2 + qb:3 + qb])
                e.then_inc(m_exped, 1)
                act.wait_ge(m_turned, h + 1)
                act.copy(pT[:, 0:2 * NP], ps[:, 3, :]).then_inc(m_copied, 1)
            with act.Fori(0, 2) as i:
                act.wait_ge(n_maxed, i + 1)
                A(sS[:, 0:NM], ps[:, 2, 0:NM], ACT.Exp, bias=stat[:, 0:1],
                  accum_out=stat[:, 2:3]).then_inc(n_exped, 1)
                act.wait_ge(n_turned, i + 1)
                act.copy(pT[:, 0:NM], ps[:, 3, 0:NM]).then_inc(n_copied, 1)
                act.wait_ge(zm_used, i * 8 + 10)
                act.copy(sS[:, NM:2 * NM], ps[:, 4, 0:MD]).then_inc(n_out, 1)
            with act.Fori(0, 2) as i:
                act.wait_ge(s_maxed, i + 1)
                A(sT[:], sT[:], ACT.Exp, bias=stat2[:, 0:1], accum_out=stat2[:, 1:2]).then_inc(s_exped, 1)
                act.wait_ge(s_turned, i + 1)
                act.copy(pTs[:], ps[:, 3, 0:G * P])
                act.copy(pTn[:], ps[0:NS, 4, 0:G * P]).then_inc(s_copied, 1)
                act.wait_ge(z_used, i * 8 + 9)
                act.copy(osb[:, 0:P], ps[:, 5, 0:P]).then_inc(s_out, 1)

            act.wait_ge(s_kept, 2)
            A(osw_hi[:], hb[:, 8:8 + HG, :], ACT.Copy).then_inc(osw_hi_done, 1)
            A(xs_hi[:, CT:2 * CT, :], hb[:, 36:44, :], ACT.Copy).then_inc(xs_hi_done, 1)
            with act.Fori(0, 2) as i:
                n = Place(OPROJ0, (20, i))
                for m in range(KT // 2):
                    for r in range(3 if m % 2 == 0 else 2):
                        split_hi(n + ((m // 2) * 5 + (0 if m % 2 == 0 else 3) + r + 4))
                    act.wait_ge(merged, i * 8 + (m + 1))
                    A(tile_view(xs2_hi, i * 8 + m), mt[:, 3, :], ACT.Copy).then_inc(merged_hi, 1)
            with act.Fori(0, OUT_BLOCKS // 4) as i:
                for r in range(4):
                    split_hi(Place(OUT0 + 4 + r, (4, i)))
            act.wait_ge(bank_free, taken(OUT_T + KT - 1))
            for c in range(4):
                if c:
                    act.wait_ge(sq_summed, 16 + c)
                A(sqh[:], acc[:, 4 * c:4 * c + 4, :], ACT.Square).then_inc(sq_done, 1)
            act.wait_ge(sq_summed, 20)
            A(rms_h[:, 0, :], ps[:, 2, 0:NT], ACT.Sqrt, bias=EPS, scale=1.0 / D).then_inc(rooted, 1)
            for c in range(4):
                act.wait_ge(normed, 11 + c)
                A(xs_hi[:, 4 * c:4 * c + 4, :], qT[:, 4 * c:4 * c + 4, :], ACT.Copy).then_inc(xs_hi_done, 1)
            with act.Fori(0, WQ_BLOCKS // 4) as i:
                for j in range(2):
                    n = Place(WQ0, (4, i))
                    split_hi(n + (2 * j + 4))
                    split_hi(n + (2 * j + 5))
                    act.copy(tile_view(qT, i * 2 + j), ps[:, j, 0:NT]).then_inc(bank_free, 1)

            def gelu(n, j, stored, before=None):
                split_hi(n + 4)
                split_hi(n + 5)
                if stored is not None:
                    act.wait_ge(act_stored[j % 2], stored)
                A(gelu_st[:, j % 2, :], ps[:, j % 2, 0:NT], ACT.Gelu_apprx_tanh).then_inc(bank_free, 1)

            def top_gates(heads):
                act.wait_ge(t_picked, heads)
                for tt in range(3):
                    e = A(ce[:, tt, :], cv[:, tt, :], ACT.Exp, bias=tz[:, tt:tt + 1],
                          accum_out=tz[:, 3 + tt:4 + tt])
                e.then_inc(t_exped, 1)

            def select(h2):
                for j in range(2 * SELECT_TILES):
                    if h2 is None:
                        gelu(Place(U0 + 2 * j), j, 16 * (j // 2) if j >= 2 else None)
                    else:
                        gelu(Place(U0 + 2 * j, (20, h2)), j, h2 * 80 + 16 * (j // 2))
                    if j % SELECT_TILES == SELECT_TILES - 2:
                        u = j // SELECT_TILES
                        top_gates(u + 1 if h2 is None else h2 * 2 + (u + 1))

            select(None)
            with act.Fori(1, PH // 2) as h2:
                select(h2)

            def spread(tb, first):
                for m in range(16):
                    k = SPREAD_U + m
                    gelu(Place(U0 + 2 * k, (32, tb)), m, tb * 128 + 16 * (k // 2))
                    if not first and m % 8 == 0:
                        act.wait_ge(gd_stored[m // 8], tb * 16)
                    act.wait_ge(hot_used, tb * 16 + (m + 3))
                    out = strided(gd[:, m // 8, :, :], 4 * (m % 8), [[1, 4], [32, PK]])
                    act.copy(out, ps[:, 2 + m % 2, :].rearrange("p (t i) -> p t i", t=4)).then_inc(g_spread, 1)

            spread(0, True)
            with act.Fori(1, NT // 64) as tb:
                spread(tb, False)

            def c_split(step, dst):
                act.wait_ge(c_made, step.value(plus=1))
                A(dst, cf[:, step.const % 2], ACT.Copy).then_inc(c_hi, 1)

            for p in range(8):
                k = LAST_U + p
                gelu(Place(U0 + 2 * k), k, 16 * (k // 2))
                c_split(Place(p), xs2_hi[:, 2 * p:2 * p + 2, :])

            def v_group(base, gg, group, dst):
                with act.Fori(0, 2) as i:
                    for p in range(4):
                        n = Place(V0 + group * 32 + 4 * p, (16, i), *([(64, gg)] if gg is not None else []))
                        for r in range(4):
                            split_hi(n + (4 + r))
                            if r == 1:
                                step = Place(8 + group * 8 + p, (4, i), *([(16, gg)] if gg is not None else []))
                                c_split(step, dst[:, bass.ds(i * 8 + 2 * p, 2), :])

            with act.Fori(0, 3) as gg:
                v_group(0, gg, 0, xs_hi)
                v_group(0, gg, 1, xs2_hi)
            v_group(0, None, 6, xs_hi)
            with act.Fori(0, 7) as i:
                for r in range(4):
                    split_hi(Place(V0 + 7 * 32 + 4 + r, (4, i)))

        @block.vector
        def _(dve):
            TT, STT, TS = dve.tensor_tensor, dve.scalar_tensor_tensor, dve.tensor_scalar

            def move(out, src):
                return TS(out, src, 1.0, None, ALU.mult)

            def split_lo(n):
                s = n.const % 4
                dve.wait_ge(hi_done, n.value(plus=1))
                TT(w_lo[:, s, :], raw[:, s, :], w_hi[:, s, :].bitcast(F32), ALU.subtract).then_inc(lo_done, 1)

            def ended(n):
                dve.wait_ge(w_released, n.value(plus=1))

            def scale_by_norm(dst, src, gain, root, cols, first, tiles):
                for k in range(first, first + tiles):
                    last = STT(out=dst[:, k, :], in0=src[:, k, :], scalar=gain[:, k:k + 1], in1=root[:, 1, 0:cols],
                               op0=ALU.mult, op1=ALU.mult)
                return last

            dve.sem_inc(bank_free, 2)
            dve.sem_inc(o_taken, 2)
            dve.memset(ones[:], 1.0).then_inc(dve_set, 1)
            dve.memset(ue[:, :, 0:CW - 1], 0.0)
            dve.wait_ge(const_loaded, 16 * 5)
            dve.wait_ge(rooted, 1)
            dve.reciprocal(rms_x[:, 1, 0:NM], rms_x[:, 0, 0:NM])
            dve.drain()
            scale_by_norm(m_raw, m_raw, gm, rms_x, NM, 0, KT).then_inc(normed, 1)
            dve.wait_ge(xs_hi_done, 1)
            TT(xs_lo[:, :, 0:NM], m_raw[:], xs_hi[:, :, 0:NM].bitcast(F32), ALU.subtract).then_inc(xs_lo_done, 1)
            for n in range(4):
                split_lo(Place(n))
            dve.wait_ge(rooted, 2)
            dve.reciprocal(rms_x[:, 1, :], rms_x[:, 0, :])
            dve.drain()
            scale_by_norm(x_raw, x_raw, g1, rms_x, NT, 0, KT).then_inc(normed, 1)
            with dve.Fori(0, MEMK_BLOCKS // 4) as i:
                for j in range(2):
                    n = Place(MEMK0 + 2 * j, (4, i))
                    split_lo(n + 4)
                    split_lo(n + 5)
                    ended(n + 1)
                    move(tile_view(mk, i * 2 + j, 0, NM), ps[:, j, 0:NM]).then_inc(bank_free, 1)
            with dve.Fori(0, 2) as i:
                n = Place(MEMV0, (8, i))
                for r in range(8):
                    split_lo(n + (r + 4))
                ended(n + 7)
                move(mv[:, :, bass.ds(i * 512, 512)], ps[:, 0:2, :]).then_inc(bank_free, 2)
            dve.wait_ge(xs_hi_done, 2)
            TT(xs_lo[:], x_raw[:], xs_hi[:].bitcast(F32), ALU.subtract).then_inc(xs_lo_done, 1)
            with dve.Fori(0, CT // 2) as i:
                for u in range(2):
                    n = Place(PROJ0 + 4 * u, (8, i))
                    for r in range(4):
                        split_lo(n + (r + 4))
                    dve.wait_ge(sig_done, i * 2 + (u + 1))
                    TT(tile_view(ue, i * 2 + u, CW - 1, NP), ps[:, 2 * u, 0:NP], sig[:, 0:NP], ALU.mult)
                    TT(ue[:, bass.ds(i * 2 + u, 1), PW:].rearrange("p o (b w) -> p (o b) w", b=NB)[:, :, CW - 1:SWD],
                       ps[:, 2 * u, NP:NT].rearrange("p (b t) -> p b t", b=NB),
                       sig[:, NP:NT].rearrange("p (b t) -> p b t", b=NB), ALU.mult).then_inc(bank_free, 2)
            with dve.Fori(0, (PROJ_BLOCKS - 4 * CT) // 4) as i:
                for r in range(4):
                    split_lo(Place(PROJ0 + 4 * CT + 4 + r, (4, i)))
            dve.wait_ge(conv_prev_loaded, 16 * CT)
            STEPS = GATE_BLOCKS // CT
            with dve.Fori(0, CT) as i:
                out_p = tile_view(cc, i, 0, NP)
                out_s = cc[:, bass.ds(i, 1), NP:NT].rearrange("p o (b t) -> p (o b) t", b=NB)
                in_s = ue[:, bass.ds(i, 1), PW:].rearrange("p o (b w) -> p (o b) w", b=NB)
                for r in range(STEPS):
                    split_lo(Place(GATE0 + 4 + r, (STEPS, i)))
                    for w in range(r * CW // STEPS, (r + 1) * CW // STEPS):
                        tap = cw[:, bass.ds(i * CW + w, 1)]
                        dve.drain()
                        if w == 0:
                            bias = cb[:, bass.ds(i, 1)]
                            TS(out_p, tile_view(ue, i, 0, NP), tap, bias, ALU.mult, ALU.add)
                            c = TS(out_s, in_s[:, :, 0:NS], tap, bias, ALU.mult, ALU.add)
                        else:
                            STT(out=out_p, in0=tile_view(ue, i, w, NP), scalar=tap, in1=out_p,
                                op0=ALU.mult, op1=ALU.add)
                            c = STT(out=out_s, in0=in_s[:, :, w:w + NS], scalar=tap, in1=out_s,
                                    op0=ALU.mult, op1=ALU.add)
                c.then_inc(conv_done, 1)

            dve.wait_ge(ln_summed, 1)
            STT(out=cc[:], in0=strided(ps[:, 2, :], 0, [[0, CT], [1, NT]]), scalar=-1.0 / CC, in1=cc[:],
                op0=ALU.mult, op1=ALU.add).then_inc(ln_centered, 1)
            dve.wait_ge(ln_rooted, 1)
            dve.reciprocal(rms_c[:, 1, :], rms_c[:, 0, :])
            dve.drain()
            TT(cc[:], cc[:], strided(rms_c[:, 1, :], 0, [[0, CT], [1, NT]]), ALU.mult).then_inc(ln_scaled, 1)
            dve.wait_ge(ln_rooted, 2)
            dve.reciprocal(gate_st[:, :, 0:NM], gate_st[:, :, 0:NM])
            dve.drain()
            for h in range(MH):
                for half in range(2):
                    t = mk[:, 2 * h + half, :]
                    last = STT(out=t, in0=t, scalar=mkg[:, half:half + 1], in1=gate_st[:, h, 0:NM],
                               op0=ALU.mult, op1=ALU.mult)
            last.then_inc(mk_ready, 1)
            dve.wait_ge(xs_hi_done, 3)
            TT(xs_lo[:, 0:CT, :], cc[:], xs_hi[:, 0:CT, :].bitcast(F32), ALU.subtract).then_inc(xs_lo_done, 1)

            for k in range(2 * G + 2):
                dve.wait_ge(rooted, 3 + k)
                if k < 2 * G:
                    g, first, gain = k // 2, (k // 2) * 12 + (k % 2) * HG, (kg if k % 2 else qg)
                    dve.reciprocal(qk_r[:], qk_r[:])
                    dve.drain()
                    last = STT(out=hb[:, first:first + HG, :], in0=hb[:, first:first + HG, :], scalar=gain[:, g:g + 1],
                               in1=qk_r[:], op0=ALU.mult, op1=ALU.mult)
                else:
                    dve.reciprocal(qk_r[:, 0:2, :], qk_r[:, 0:2, :])
                    dve.drain()
                    for half in range(2):
                        first = 36 + (k - 2 * G) * HG + half
                        t = hb[:, first:first + 3:2, :]
                        last = STT(out=t, in0=t, scalar=mqg[:, half:half + 1], in1=qk_r[:, 0:2, :],
                                   op0=ALU.mult, op1=ALU.mult)
                last.then_inc(normed, 1)

            for g in range(G):
                for f in range(4):
                    m = 4 * g + f
                    dve.wait_ge(vt_turned, m + 1)
                    if f < 2:
                        dst = vnp[:, f, g * HG:(g + 1) * HG, :].rearrange("p h d -> p (h d)")
                        src = ps[:, 2 + f, :]
                    else:
                        dst = nnew[:, f - 2, g * HG * P:(g + 1) * HG * P]
                        src = ps[0:NB * NS, 2 + f, :]
                    dve.tensor_copy(dst, src).then_inc(vt_copied, 1)

            def negmax(out, src):
                return dve.tensor_reduce(out, src, AX.X, ALU.max, negate=True)

            dve.wait_ge(dist_p_loaded, 16)
            dve.wait_ge(vp_stored, 0 + 16)
            with dve.Fori(0, HG) as h:
                dve.tensor_copy(q_st[:], hb[:, 0:36, :].rearrange("p (g k) n -> p g k n", g=G)[
                    :, :, bass.ds(h, 1), 0:NP].rearrange("p g o n -> p (g o) n"))
                for st in range(2):
                    last = dve.tensor_copy(v_st[:, st], vnp[:, st].rearrange("p (g h) d -> p g h d", g=G)[
                        :, :, bass.ds(h, 1), :].rearrange("p g o d -> p (g o) d"))
                last.then_inc(a_staged, 1)
                dve.wait_ge(a_scored, h + 1)
                for g in range(G):
                    m = slope[:, bass.ds(h + g * HG, 1)]
                    STT(out=sS[:, g * P:(g + 1) * P], in0=dpr[:, 0, g, 0:P], scalar=m,
                        in1=ps[:, 2, g * P:(g + 1) * P], op0=ALU.mult, op1=ALU.add)
                    src = ps[:, 3 + g // 2, (g % 2) * NP:(g % 2 + 1) * NP]
                    STT(out=sS[:, G * P + g * NP:G * P + (g + 1) * NP], in0=dpr[:, 1, g, :], scalar=m, in1=src,
                        op0=ALU.mult, op1=ALU.add)
                dve.drain()
                negmax(stat[:, 0:1], sS[:, 0:G * P])
                negmax(stat[:, 1:2], sS[:, G * P:G * (P + NP)]).then_inc(a_biased, 1)
                dve.wait_ge(a_exped, h + 1)
                dve.reciprocal(stat[:, 4:6], stat[:, 2:4])
                dve.drain()
                TS(sS[:, 0:G * P], sS[:, 0:G * P], stat[:, 4:5], None, ALU.mult)
                TS(sS[:, G * P:G * (P + NP)], sS[:, G * P:G * (P + NP)], stat[:, 5:6], None, ALU.mult
                   ).then_inc(a_probs, 1)
                dve.wait_ge(a_mixed, h + 1)
                move(tile_view(hb, h + 8, 0, NP), ps[:, 2, 0:NP]).then_inc(a_kept, 1)

            dve.wait_ge(km_loaded[1], 16)
            with dve.Fori(0, MH) as h:
                dve.tensor_copy(mq_st[:], hb[:, bass.ds(h * 2 + 36, 2), 0:NP])
                dve.tensor_copy(mv_st[:], km[:, 1, :].rearrange("p (s n) -> p s n", s=2)[:, :, bass.ds(h * MD, MD)]
                                ).then_inc(m_staged, 1)
                dve.wait_ge(m_scored, h + 1)
                negmax(stat[:, 0:2], ps[:, 2, :].rearrange("p (q n) -> p q n", q=2)).then_inc(m_maxed, 1)
                dve.wait_ge(m_exped, h + 1)
                dve.reciprocal(stat[:, 4:6], stat[:, 2:4])
                dve.drain()
                TS(sS[:, 0:NM], sS[:, 0:NM], stat[:, 4:5], None, ALU.mult)
                TS(sS[:, NM:2 * NM], sS[:, NM:2 * NM], stat[:, 5:6], None, ALU.mult).then_inc(m_probs, 1)
                dve.wait_ge(m_mixed, h + 1)
                move(hb[:, bass.ds(h * 2 + 36, 2), 0:NP],
                                ps[:, 4, :].rearrange("p (d n) -> p d n", d=2)).then_inc(m_kept, 1)

            dve.memset(zm[:], 0.0)
            dve.drain()
            with dve.Fori(0, 2) as i:
                def mask_memory(part, bq, src_of):
                    dve.wait_ge(zm_used, i * 8 + (part * 4 + bq + 2))
                    for half in range(2):
                        last = move(strided(zm[:, half, :, :], 0, [[DIAG, MH], [1, NS]]), src_of(half))
                    last.then_inc(zm_set, 1)

                for bq in range(4):
                    mask_memory(0, bq, lambda half: hb[:, 36 + half:43 + half:2, bass.ds(i * 32 + (NP + NS * bq), NS)])
                dve.wait_ge(zm_used, i * 8 + 6)
                negmax(stat[:, 0:1], ps[:, 2, 0:NM]).then_inc(n_maxed, 1)
                dve.wait_ge(n_exped, i + 1)
                dve.reciprocal(stat[:, 4:5], stat[:, 2:3])
                dve.drain()
                TS(sS[:, 0:NM], sS[:, 0:NM], stat[:, 4:5], None, ALU.mult).then_inc(n_probs, 1)
                dve.wait_ge(n_copied, i + 1)
                for bq in range(4):
                    mask_memory(1, bq, lambda half: pT[:, half * P + 32 * bq:half * P + 32 * bq + 32].rearrange(
                        "p (h t) -> p h t", h=MH))
                dve.wait_ge(n_back, i + 1)
                for dt in range(2):
                    last = move(
                        hb[:, 36 + dt:43 + dt:2, bass.ds(i * 32 + NP, 32)].rearrange("p h (b t) -> p b h t", b=4),
                        ps[:, 5, dt * P:(dt + 1) * P].rearrange("p (b h t) -> p b h t", b=4, h=MH))
                last.then_inc(n_kept, 1)

            dve.wait_ge(vp_stored, 16)
            dve.wait_ge(new_stored, 32)
            dve.memset(z[:], 0.0)
            dve.memset(zn[:], 0.0)
            dve.wait_ge(dist_s_loaded, 16)
            dve.drain()
            with dve.Fori(0, 2) as i:
                for bq in range(4):
                    cols = bass.ds(i * 32 + (NP + NS * bq), NS)
                    dve.wait_ge(z_used, i * 8 + (bq + 1))
                    for dst, src in z_views(z, lambda g: hb[:, g * 12:g * 12 + HG, cols]):
                        move(dst, src)
                    for g in (1, 2):
                        dve.tensor_copy(strided(z[:, :, :, :], (UNITS + g - 1) * ZU, [[DIAG, HG], [1, NS]]),
                                        hb[:, g * 12:g * 12 + HG, cols])
                    dve.tensor_copy(kn[:].rearrange("p (g h) t -> p g h t", g=G),
                                    hb[:, 0:36, :].rearrange("p (g k) n -> p g k n", g=G)[:, :, HG:2 * HG, cols]
                                    ).then_inc(z_set, 1)
                dve.wait_ge(z_used, i * 8 + 5)
                TT(sT[:], ps[:, 2, 0:SAMPLE_COLS], dsm[:], ALU.add)
                dve.drain()
                negmax(stat2[:, 0:1], sT[:]).then_inc(s_maxed, 1)
                dve.wait_ge(s_exped, i + 1)
                dve.reciprocal(stat2[:, 2:3], stat2[:, 1:2])
                dve.drain()
                TS(sT[:], sT[:], stat2[:, 2:3], None, ALU.mult).then_inc(s_probs, 1)
                dve.wait_ge(s_copied, i + 1)
                for bq in range(4):
                    def probs_of(g):
                        return pTs[:, g * P + 32 * bq:g * P + 32 * bq + 32].rearrange("p (h t) -> p h t", h=HG)

                    dve.wait_ge(z_used, i * 8 + (4 + bq + 1))
                    for dst, src in z_views(z, probs_of):
                        dve.tensor_copy(dst, src)
                    dve.tensor_copy(strided(zn[:, :, :, :], 0, [[HG * 32, G], [DIAG, HG], [1, NS]]),
                                    strided(pTn[:], 32 * bq, [[P, G], [NS, HG], [1, NS]])).then_inc(z_set, 1)
                dve.wait_ge(s_back, i + 1)
                move(hb[:, 8:8 + HG, bass.ds(i * 32 + NP, 32)].rearrange("p h (b t) -> p b h t", b=4),
                                ps[:, 6, 0:P].rearrange("p (b h t) -> p b h t", b=4, h=HG)).then_inc(s_kept, 1)

            dve.wait_ge(osw_hi_done, 1)
            TT(osw_lo[:], hb[:, 8:8 + HG, :], osw_hi[:].bitcast(F32), ALU.subtract).then_inc(osw_lo_done, 1)
            dve.wait_ge(xs_hi_done, 4)
            TT(xs_lo[:, CT:2 * CT, :], hb[:, 36:44, :], xs_hi[:, CT:2 * CT, :].bitcast(F32), ALU.subtract
               ).then_inc(xs_lo_done, 1)
            with dve.Fori(0, 2) as i:
                n = Place(OPROJ0, (20, i))
                for m in range(KT // 2):
                    blocks = range(3) if m % 2 == 0 else range(3, 5)
                    for r in blocks:
                        split_lo(n + ((m // 2) * 5 + r + 4))
                    ended(n + ((m // 2) * 5 + blocks[-1]))
                    dve.wait_ge(gl_loaded[m % 2], i * 64 + 16 * (m // 2 + 1))
                    u = m % 2
                    TT(mt[:, 0, :], gl[:, u, 0, :], ps[:, 2 + 3 * u, 0:NT], ALU.mult)
                    TT(mt[:, 1, :], gl[:, u, 1, :], ps[:, 4 + 3 * u, 0:NT], ALU.mult)
                    TT(mt[:, 2, :], gl[:, u, 2, :], ps[:, 3 + 3 * u, 0:NT], ALU.mult).then_inc(o_taken, 1)
                    dve.drain()
                    TT(mt[:, 0, :], mt[:, 0, :], mt[:, 1, :], ALU.add)
                    dve.drain()
                    TT(mt[:, 3, :], mt[:, 0, :], mt[:, 2, :], ALU.add).then_inc(merged, 1)
                    dve.wait_ge(merged_hi, i * 8 + (m + 1))
                    TT(tile_view(xs2_lo, i * 8 + m), mt[:, 3, :], tile_view(xs2_hi, i * 8 + m).bitcast(F32),
                       ALU.subtract).then_inc(merged_lo, 1)

            def add_tiles(n, m):
                split_lo(n + 4)
                split_lo(n + 5)
                ended(n + 1)
                t = tile_view(acc, m)
                TT(t, t, ps[:, (n.const // 2) % 2, 0:NT], ALU.add).then_inc(bank_free, 1)

            dve.wait_ge(acc_loaded, 16)
            with dve.Fori(0, OUT_BLOCKS // 4) as i:
                for j in range(2):
                    add_tiles(Place(OUT0 + 2 * j, (4, i)), i * 2 + j)
            dve.wait_ge(rooted, 11)
            dve.reciprocal(rms_h[:, 1, :], rms_h[:, 0, :])
            dve.drain()
            for c in range(4):
                scale_by_norm(qT, acc, g2, rms_h, NT, 4 * c, 4).then_inc(normed, 1)
            for c in range(4):
                part = slice(4 * c, 4 * c + 4)
                dve.wait_ge(xs_hi_done, 5 + c)
                TT(xs_lo[:, part, :], qT[:, part, :], xs_hi[:, part, :].bitcast(F32), ALU.subtract
                   ).then_inc(xs_lo_done, 1)
            with dve.Fori(0, WQ_BLOCKS // 4) as i:
                for r in range(4):
                    split_lo(Place(WQ0 + 4 + r, (4, i)))

            def select(n, h):
                dve.tensor_copy(pq_st[:], qT[:, bass.ds(h * 2, 2), :]).then_inc(t_staged, 1)
                split_lo(n + 4)
                split_lo(n + 5)
                split_lo(n + 6)
                dve.wait_ge(t_scored, h + 1)
                split_lo(n + 7)
                six = [slice(q * PK, (q + 1) * PK) for q in range(6)]
                scores = [ps[:, 2 + q // 3, (q % 3) * PK:(q % 3 + 1) * PK] for q in range(6)]
                for q in range(6):
                    dve.max(tv[:, q, 0:8], scores[q])
                dve.drain()
                for q in range(6):
                    dve.max_index(tiu[:, q, 0:8], tv[:, q, 0:8], scores[q])
                    dve.match_replace(tW[:, six[q]], tv[:, q, 0:8], scores[q], -3.0e38)
                dve.drain()
                for q in range(6):
                    dve.max(tv[:, q, 8:16], tW[:, six[q]])
                dve.drain()
                split_lo(n + 8)
                split_lo(n + 9)
                for q in range(6):
                    dve.max_index(tiu[:, q, 8:16], tv[:, q, 8:16], tW[:, six[q]])
                TT(tS[:].rearrange("p (t a b) -> p t a b", t=3, a=TOPK),
                   strided(tv[:, :, :], 0, [[2 * TOPK, 3], [1, TOPK], [0, TOPK]]),
                   strided(tv[:, :, :], TOPK, [[2 * TOPK, 3], [0, TOPK], [1, TOPK]]), ALU.add)
                dve.drain()
                dve.tensor_copy(tif[:], tiu[:])
                three = [slice(t * 2 * PK, (t + 1) * 2 * PK) for t in range(3)]
                for t in range(3):
                    dve.max(cv[:, t, 0:8], tS[:, three[t]])
                dve.drain()
                TS(tz[:, 0:3], cv[:, :, 0], -1.0, None, ALU.mult)
                for t in range(3):
                    dve.max_index(ci[:, t, 0:8], cv[:, t, 0:8], tS[:, three[t]])
                    dve.match_replace(tW[:, three[t]], cv[:, t, 0:8], tS[:, three[t]], -3.0e38)
                dve.drain()
                for t in range(3):
                    last = dve.max(cv[:, t, 8:16], tW[:, three[t]])
                last.then_inc(t_picked, 1)
                dve.drain()
                for t in range(3):
                    dve.max_index(ci[:, t, 8:16], cv[:, t, 8:16], tW[:, three[t]])
                dve.drain()
                split_lo(n + 10)
                split_lo(n + 11)
                TS(cab[:, 0], ci[:], 4, None, ALU.logical_shift_right)
                TS(cab[:, 1], ci[:], TOPK - 1, None, ALU.bitwise_and)
                dve.drain()
                dve.tensor_copy(cabf[:], cab[:])
                dve.drain()
                for half in range(2):
                    TT(eq[:], strided(iota16[:, :], 0, [[0, 3], [0, TOPK], [1, TOPK]]),
                       strided(cabf[:, :, :, :], half * 3 * TOPK, [[TOPK, 3], [1, TOPK], [0, TOPK]]), ALU.is_equal)
                    dve.drain()
                    TT(eq[:], eq[:], strided(tif[:, :, :], half * TOPK, [[2 * TOPK, 3], [0, TOPK], [1, TOPK]]),
                       ALU.mult)
                    dve.drain()
                    dve.tensor_reduce(R[:, :, half, bass.ds(h, 1), :].rearrange("p t o k -> p t (o k)"), eq[:],
                                      AX.X, ALU.add)
                    dve.drain()
                split_lo(n + 12)
                split_lo(n + 13)
                dve.wait_ge(t_exped, h + 1)
                dve.reciprocal(tz[:, 6:9], tz[:, 3:6])
                dve.drain()
                TT(R[:, :, 2, bass.ds(h, 1), :].rearrange("p t o k -> p t (o k)"), ce[:],
                   strided(tz[:, :], 6, [[1, 3], [0, TOPK]]), ALU.mult).then_inc(r_done, 1)

            dve.wait_ge(bank_free, taken(WQ_T + KT - 1))
            with dve.Fori(0, PH // 2) as h2:
                for u in range(2):
                    select(Place(U0 + 2 * SELECT_TILES * u, (4 * SELECT_TILES, h2)), h2 * 2 + u)

            dve.wait_ge(r_turned, 1)
            dve.tensor_copy(T[:, :, 0:P], ps[:, 2, 0:3 * P].rearrange("p (k n) -> p k n", k=3))
            dve.tensor_copy(T[:, :, P:2 * P], ps[:, 3, 0:3 * P].rearrange("p (k n) -> p k n", k=3))
            dve.tensor_copy(T[:, :, 2 * P:NT], ps[:, 4, 0:3 * P].rearrange("p (k n) -> p k n", k=3)[:, :, 2 * P - 192:P]
                            ).then_inc(t_set, 1)
            dve.drain()
            with dve.Fori(0, NT // 64) as tb:
                for m in range(16):
                    n = Place(U0 + 2 * SPREAD_U + 2 * m, (32, tb))
                    dve.wait_ge(hot_used, tb * 16 + (m + 1))
                    for tk in range(4):
                        tok = bass.ds(tb * 64 + (4 * m + tk), 1)
                        TS(hot[:, m % 2, tk, 0, :], iota[:], T[:, 0, tok], None, ALU.is_equal)
                        last = TS(hot[:, m % 2, tk, 1, :], iota[:], T[:, 1, tok], T[:, 2, tok],
                                  ALU.is_equal, ALU.mult)
                    last.then_inc(hot_set, 1)
                    split_lo(n + 4)
                    split_lo(n + 5)

            def c_make(step, loaded):
                p = step.const % 8
                c, ii = (p // 2) % 2, 2 * (p % 2)
                dve.wait_ge(chunk_loaded[c], loaded.value(32, 32))
                dve.wait_ge(c_hi, step.value(plus=-1)) if step.const >= 2 else None
                TT(cf[:, p % 2].rearrange("p i (b t) -> p i b t", t=32),
                   actc[:, c, ii:ii + 2, :].rearrange("p i (b t) -> p i b t", t=32),
                   gc[:, c, :, ii:ii + 2, :].rearrange("p b i t -> p i b t"), ALU.mult).then_inc(c_made, 1)

            def c_rest(step, hi, lo):
                dve.wait_ge(c_hi, step.value(plus=1))
                TT(lo, cf[:, step.const % 2], hi.bitcast(F32), ALU.subtract).then_inc(c_lo, 1)

            for p in range(8):
                n = Place(U0 + 2 * (LAST_U + p))
                split_lo(n + 4)
                split_lo(n + 5)
                c_make(Place(p), Place(p // 4))
                c_rest(Place(p), xs2_hi[:, 2 * p:2 * p + 2, :], xs2_lo[:, 2 * p:2 * p + 2, :])

            def v_group(gg, group, hi, lo):
                def at(const, per_i, per_gg, i):
                    return Place(const, (per_i, i), *([(per_gg, gg)] if gg is not None else []))

                with dve.Fori(0, 2) as i:
                    for p in range(4):
                        n = at(V0 + group * 32 + 4 * p, 16, 64, i)
                        step = at(8 + group * 8 + p, 4, 16, i)
                        two = bass.ds(i * 8 + 2 * p, 2)
                        split_lo(n + 4)
                        split_lo(n + 5)
                        c_make(step, at(2 + 2 * group, 1, 4, i))
                        ended(n + 1)
                        t = tile_view(acc, i * 8 + 2 * p)
                        TT(t, t, ps[:, 0, 0:NT], ALU.add).then_inc(bank_free, 1)
                        split_lo(n + 6)
                        split_lo(n + 7)
                        c_rest(step, hi[:, two, :], lo[:, two, :])
                        ended(n + 3)
                        t = tile_view(acc, i * 8 + 2 * p + 1)
                        TT(t, t, ps[:, 1, 0:NT], ALU.add).then_inc(bank_free, 1)
                dve.drain()

            with dve.Fori(0, 3) as gg:
                v_group(gg, 0, xs_hi, xs_lo)
                v_group(gg, 1, xs2_hi, xs2_lo)
            v_group(None, 6, xs_hi, xs_lo)
            with dve.Fori(0, 7) as i:
                for j in range(2):
                    add_tiles(Place(V0 + 7 * 32 + 2 * j, (4, i)), i * 2 + j)
            for j in range(2):
                ended(Place(END - 4 + 2 * j + 1))
                TT(acc[:, KT - 2 + j, :], acc[:, KT - 2 + j, :], ps[:, j, 0:NT], ALU.add).then_inc(bank_free, 1)

        @block.tensor
        def _(pe):
            def three(out, a_hi, a_lo, b_hi, b_lo, start, stop):
                pe.matmul(out, a_hi, b_hi, start=start, stop=False)
                pe.matmul(out, a_hi, b_lo, start=False, stop=False)
                return pe.matmul(out, a_lo, b_hi, start=False, stop=stop)

            def stream(n, out, hi, lo, first, start, stop, cols=NT, tiles=8, at=0):
                s = n.const % 4
                for k in range(tiles):
                    w = slice((at + k) * P, (at + k + 1) * P)
                    last = three(out, w_hi[:, s, w], w_lo[:, s, w], hi[:, first + k, 0:cols], lo[:, first + k, 0:cols],
                                 start and k == 0, stop and k == tiles - 1)
                return last

            def split_done(n):
                pe.wait_ge(lo_done, n.value(plus=1))

            def project(n, tile, bank, hi, lo, cols=NT):
                pe.wait_ge(bank_free, tile.value(plus=1))
                for half in range(2):
                    split_done(n + half)
                    stream(n + half, ps[:, bank, 0:cols], hi, lo, 8 * half, half == 0, half == 1, cols
                           ).then_inc(w_released, 1)

            pe.sem_inc(kv_used, 4)
            pe.sem_inc(hot_used, 2)
            pe.sem_inc(zm_used, 2)
            pe.sem_inc(z_used, 1)
            pe.wait_ge(dve_set, 1)

            def sum_squares(count, src, bank, cols):
                for c in range(4):
                    pe.wait_ge(sq_done, count + c + 1)
                    for k in range(4):
                        last = pe.matmul(ps[:, bank, 0:cols], ones[:], src[:, k, 0:cols],
                                         start=c == 0 and k == 0, stop=c == 3 and k == 3)
                    last.then_inc(sq_summed, 1)

            sum_squares(0, sq4, 2, NM)
            sum_squares(4, sq4, 3, NT)
            pe.wait_ge(xs_lo_done, 1)
            with pe.Fori(0, MEMK_BLOCKS // 4) as i:
                for j in range(2):
                    project(Place(MEMK0 + 2 * j, (4, i)), Place(MEMK_T + j, (2, i)), j, xs_hi, xs_lo, NM)
            with pe.Fori(0, 2) as i:
                pe.wait_ge(bank_free, i * 2 + (MEMV_T + 2))
                for r in range(8):
                    n = Place(MEMV0 + r, (8, i))
                    split_done(n)
                    for kk in range(2):
                        k, w = 2 * r + kk, slice(kk * 512, (kk + 1) * 512)
                        for tt in range(2):
                            t = slice(tt * P, (tt + 1) * P)
                            last = three(ps[:, tt, :], xs_hi[:, k, t], xs_lo[:, k, t], w_hi[:, r % 4, w],
                                         w_lo[:, r % 4, w], k == 0, k == KT - 1)
                    last.then_inc(w_released, 1)
            pe.wait_ge(xs_lo_done, 2)
            pe.wait_ge(bank_free, taken(PROJ_T - 1))
            with pe.Fori(0, CT // 2) as i:
                for j in range(4):
                    project(Place(PROJ0 + 2 * j, (8, i)), Place(PROJ_T - 2 + j, (4, i)), j, xs_hi, xs_lo)
            with pe.Fori(0, (PROJ_BLOCKS + GATE_BLOCKS) // 4 - CT) as i:
                for j in range(2):
                    project(Place(PROJ0 + 4 * CT + 2 * j, (4, i)), Place(PROJ_T + 2 * CT + j, (2, i)), j, xs_hi, xs_lo)

            pe.wait_ge(conv_done, CT)
            for ct in range(CT):
                last = pe.matmul(ps[:, 2, 0:NT], ones[:], cc[:, ct, :], start=ct == 0, stop=ct == CT - 1)
            last.then_inc(ln_summed, 1)
            for c in range(2):
                pe.wait_ge(ln_squared, c + 1)
                for k in range(4):
                    last = pe.matmul(ps[:, 3, 0:NT], ones[:], gate_st[:, k, :],
                                     start=c == 0 and k == 0, stop=c == 1 and k == 3)
                last.then_inc(ln_summed, 1)
            for c in range(2):
                pe.wait_ge(ln_squared, 2 + c + 1)
                for h in range(2):
                    for half in range(2):
                        last = pe.matmul(ps[:, 4 + c, h * NM:(h + 1) * NM], ones[:], gate_st[:, 2 * h + half, 0:NM],
                                         start=half == 0, stop=half == 1)
                last.then_inc(ln_summed, 1)
            for k in range(2 * G + 2):
                pe.wait_ge(sq_done, 8 + k + 1)
                for t in range(HG):
                    if k < 2 * G:
                        last = pe.matmul(ps[:, 2 + t, 0:NT], ones[:], qk_sq[:, t, :], start=True, stop=True)
                    else:
                        last = pe.matmul(ps[:, 2 + t // 2, 0:NT], ones[:], qk_sq[:, t, :],
                                         start=t % 2 == 0, stop=t % 2 == 1)
                last.then_inc(sq_summed, 1)

            pe.wait_ge(normed, 2 + 2 * G + 2)
            for g in range(G):
                for f in range(4):
                    m = 4 * g + f
                    if m >= 4:
                        pe.wait_ge(vt_copied, m - 3)
                    for h in range(HG):
                        tile = g * 12 + (4 if f == 2 else 8) + h
                        cols = slice(f * P, (f + 1) * P) if f < 2 else slice(NP, NT)
                        rows = cols.stop - cols.start
                        last = pe.transpose(ps[0:rows, 2 + f, h * P:(h + 1) * P], hb[:, tile, cols], ident[:])
                    last.then_inc(vt_turned, 1)

            with pe.Fori(0, HG) as h:
                pe.wait_ge(a_staged, h + 1)
                for g in range(G):
                    def keys(n):
                        return hb[:, bass.ds(h + (g * 12 + HG), 1), 0:n].rearrange("p o n -> p (o n)")

                    pe.matmul(ps[:, 2, g * P:(g + 1) * P], q_st[:, g, 0:P], keys(P), start=True, stop=True)
                    last = pe.matmul(ps[:, 3 + g // 2, (g % 2) * NP:(g % 2 + 1) * NP], q_st[:, g, P:NP], keys(NP),
                                     start=True, stop=True)
                last.then_inc(a_scored, 1)
                pe.wait_ge(a_probs, h + 1)
                for g in range(G):
                    pe.transpose(ps[:, 5, g * P:(g + 1) * P], sS[:, g * P:(g + 1) * P], ident[:])
                for c in range(2 * G):
                    src = sS[:, (G + c) * P:(G + c + 1) * P]
                    last = pe.transpose(ps[:, 6 + c // 3, (c % 3) * P:(c % 3 + 1) * P], src, ident[:])
                last.then_inc(a_turned, 1)
                pe.wait_ge(a_copied, h + 1)
                for g in range(G):
                    pe.matmul(ps[:, 2, 0:P], v_st[:, 0, g, :], pT[:, g * P:(g + 1) * P], start=g == 0, stop=g == G - 1)
                for c in range(2 * G):
                    last = pe.matmul(ps[:, 2, P:NP], v_st[:, c % 2, c // 2, :], pT[:, (G + c) * P:(G + c + 1) * P],
                                     start=c == 0, stop=c == 2 * G - 1)
                last.then_inc(a_mixed, 1)

            pe.wait_ge(km_loaded[0], 16)
            with pe.Fori(0, MH) as h:
                pe.wait_ge(m_staged, h + 1)
                for qb in range(2):
                    for half in range(2):
                        last = pe.matmul(ps[:, 2, qb * NM:(qb + 1) * NM], mq_st[:, half, qb * P:(qb + 1) * P],
                                         km[:, 0, bass.ds(h * (2 * NM) + half * NM, NM)],
                                         start=half == 0, stop=half == 1)
                last.then_inc(m_scored, 1)
                pe.wait_ge(m_probs, h + 1)
                for qb in range(2):
                    for st in range(2):
                        last = pe.transpose(ps[:, 3, st * NP + qb * P:st * NP + (qb + 1) * P],
                                            sS[:, qb * NM + st * P:qb * NM + (st + 1) * P], ident[:])
                last.then_inc(m_turned, 1)
                pe.wait_ge(m_copied, h + 1)
                for dt in range(2):
                    for st in range(2):
                        last = pe.matmul(ps[:, 4, dt * NP:(dt + 1) * NP], mv_st[:, st, dt * P:(dt + 1) * P],
                                         pT[:, st * NP:(st + 1) * NP], start=st == 0, stop=st == 1)
                last.then_inc(m_mixed, 1)

            with pe.Fori(0, 2) as i:
                for part in range(2):
                    for bq in range(4):
                        c = part * 4 + bq
                        pe.wait_ge(km_loaded[bq % 2], i * 64 + 16 * (c // 2 + 2))
                        pe.wait_ge(zm_set, i * 8 + (c + 1))
                        for h in range(MH):
                            for half in range(2):
                                at = (2 * h + half) * NM if part == 0 else half * MH * MD + h * MD
                                last = pe.matmul(ps[32 * bq:32 * bq + 32, 2 + 2 * part, 0:NM], zm[:, half, h, :],
                                                 km[:, bq % 2, at:at + NM], start=h == 0 and half == 0,
                                                 stop=h == MH - 1 and half == 1, tile_position=(0, 32 * bq))
                        last.then_inc(zm_used, 1)
                    if part == 0:
                        pe.wait_ge(n_probs, i + 1)
                        for st in range(2):
                            last = pe.transpose(ps[:, 3, st * P:(st + 1) * P], sS[:, st * P:(st + 1) * P], ident[:])
                        last.then_inc(n_turned, 1)
                pe.wait_ge(n_out, i + 1)
                for dt in range(2):
                    last = pe.transpose(ps[:, 5, dt * P:(dt + 1) * P], sS[:, NM + dt * P:NM + (dt + 1) * P], ident[:])
                last.then_inc(n_back, 1)

            GROUP_OF = [g for g in range(G) for _ in range(min(DILATIONS[g], NS))]
            with pe.Fori(0, 2) as i:
                for part in range(2):
                    for bq in range(4):
                        rows = slice(32 * bq, 32 * bq + 32)
                        where = (0, 32 * bq)
                        c = part * 4 + bq
                        if part:
                            pe.wait_ge(vnew_loaded, i * 64 + 16 * (bq + 1))
                        pe.wait_ge(z_set, i * 8 + (c + 1))
                        for u in range(UNITS):
                            m = c * UNITS + u
                            g = GROUP_OF[u]
                            pe.wait_ge(kv_loaded[m % 4], i * (16 * 2 * UNITS) + 16 * (m // 4 + 1))
                            for h in range(HG):
                                kv_h = kv[:, m % 4, h * P:(h + 1) * P]
                                if part == 0:
                                    first = h == 0 and (u == 0 or GROUP_OF[u - 1] != g)
                                    final = h == HG - 1 and (u == UNITS - 1 or GROUP_OF[u + 1] != g)
                                    last = pe.matmul(ps[rows, 2, g * P:(g + 1) * P], z[:, u, h, :], kv_h,
                                                     start=first, stop=final, tile_position=where)
                                else:
                                    last = pe.matmul(ps[rows, 5, 0:P], z[:, u, h, :], kv_h,
                                                     start=u == 0 and h == 0, stop=False, tile_position=where)
                            last.then_inc(kv_used, 1)
                        for g in range(G):
                            for h in range(HG):
                                if part == 0:
                                    at = G * P + g * NS
                                    last = pe.matmul(ps[rows, 2, at:at + NS], z[:, UNITS + g - 1 if g else 0, h, :],
                                                     kn[:, g * HG + h, :], start=h == 0, stop=h == HG - 1,
                                                     tile_position=where)
                                else:
                                    last = pe.matmul(ps[rows, 5, 0:P], zn[:, g, h, :],
                                                     vnew[:, (g * HG + h) * P:(g * HG + h + 1) * P], start=False,
                                                     stop=g == G - 1 and h == HG - 1, tile_position=where)
                        last.then_inc(z_used, 1)
                    if part == 0:
                        pe.wait_ge(s_probs, i + 1)
                        for g in range(G):
                            pe.transpose(ps[:, 3, g * P:(g + 1) * P], sT[:, g * P:(g + 1) * P], ident[:])
                        for g in range(G):
                            last = pe.transpose(ps[0:NS, 4, g * P:(g + 1) * P],
                                                sT[:, G * P + g * NS:G * P + (g + 1) * NS], ident[:])
                        last.then_inc(s_turned, 1)
                pe.wait_ge(s_out, i + 1)
                pe.transpose(ps[:, 6, 0:P], osb[:, 0:P], ident[:]).then_inc(s_back, 1)

            pe.wait_ge(bank_free, taken(GATE_T + 3 * KT - 1))
            pe.wait_ge(xs_lo_done, 4)
            pe.wait_ge(osw_lo_done, 1)
            with pe.Fori(0, 2) as i:
                for pair in range(KT // 4):
                    n = Place(OPROJ0 + 5 * pair, (20, i))
                    for u in range(2):
                        pe.wait_ge(o_taken, i * 8 + (2 * pair + u + 1))
                        if u:
                            split_done(n + 2)
                            for v in range(2):
                                last = stream(n + 2, ps[:, 4 + 3 * v, 0:NT], osw_hi, osw_lo, 0, True, True,
                                              tiles=4, at=4 * v)
                            last.then_inc(w_released, 1)
                        for branch in range(2):
                            r = 3 * u + branch
                            split_done(n + r)
                            stream(n + r, ps[:, 2 + 3 * u + branch, 0:NT], xs_hi, xs_lo, 8 * branch, True, True
                                   ).then_inc(w_released, 1)
            pe.wait_ge(merged_lo, KT)
            with pe.Fori(0, OUT_BLOCKS // 4) as i:
                for j in range(2):
                    project(Place(OUT0 + 2 * j, (4, i)), Place(OUT_T + j, (2, i)), j, xs2_hi, xs2_lo)
            sum_squares(16, sqh, 2, NT)
            pe.wait_ge(xs_lo_done, 8)
            with pe.Fori(0, WQ_BLOCKS // 4) as i:
                for j in range(2):
                    project(Place(WQ0 + 2 * j, (4, i)), Place(WQ_T + j, (2, i)), j, xs_hi, xs_lo)
            with pe.Fori(0, PH // 2) as h2:
                for j in range(2 * SELECT_TILES):
                    project(Place(U0 + 2 * j, (4 * SELECT_TILES, h2)), Place(U_T + j, (2 * SELECT_TILES, h2)), j % 2,
                            xs_hi, xs_lo)
                    if j % SELECT_TILES == 0:
                        pe.wait_ge(t_staged, h2 * 2 + (j // SELECT_TILES + 1))
                        for t in range(3):
                            tok = min(t * P, NT - P)
                            for half, keys in enumerate((k1T, k2T)):
                                q = 2 * t + half
                                last = pe.matmul(ps[:, 2 + q // 3, (q % 3) * PK:(q % 3 + 1) * PK],
                                                 pq_st[:, half, tok:tok + P], keys, start=True, stop=True)
                        last.then_inc(t_scored, 1)
            pe.wait_ge(r_done, PH)
            for t in range(3):
                for kind in range(3):
                    last = pe.transpose(ps[:, 2 + t, kind * P:(kind + 1) * P],
                                        R[:, t, kind, :, :].rearrange("p h k -> p (h k)"), ident[:])
            last.then_inc(r_turned, 1)
            pe.wait_ge(t_set, 1)
            with pe.Fori(0, NT // 64) as tb:
                for m in range(16):
                    project(Place(U0 + 2 * (SPREAD_U + m), (32, tb)), Place(U_T + SPREAD_U + m, (16, tb)), m % 2,
                            xs_hi, xs_lo)
                    pe.wait_ge(hot_set, tb * 16 + (m + 1))
                    pe.wait_ge(g_spread, tb * 16 + (m + 1))
                    for tk in range(4):
                        last = pe.matmul(ps[:, 2 + m % 2, tk * PK:(tk + 1) * PK], hot[:, m % 2, tk, 0, :],
                                         hot[:, m % 2, tk, 1, :], start=True, stop=True)
                    last.then_inc(hot_used, 1)
            with pe.Fori(0, 4) as p:
                for j in range(2):
                    project(Place(U0 + 2 * (LAST_U + j), (4, p)), Place(U_T + LAST_U + j, (2, p)), j, xs_hi, xs_lo)
            with pe.Fori(0, 4) as gg:
                for group, (hi, lo) in enumerate(((xs2_hi, xs2_lo), (xs_hi, xs_lo))):
                    with pe.Fori(0, 8) as i:
                        pe.wait_ge(c_lo, gg * 16 + 8 * (group + 1))
                        for j in range(2):
                            project(Place(V0 + 32 * group + 2 * j, (4, i), (64, gg)),
                                    Place(V_T + 16 * group + j, (2, i), (32, gg)), j, hi, lo)


_CONV_COLS = CT * CW


def _lay_out(inp):
    import numpy as np

    a = {}

    def c(x):
        return np.ascontiguousarray(x)

    def features(x):
        return c(x.T.reshape(-1, P, x.shape[0]).transpose(1, 0, 2))

    def vec(x):
        return x.reshape(-1, P).T

    def col_tiles(w):
        k, n = w.shape
        return c(w.reshape(k // (8 * P), 8, P, n // P, P).transpose(3, 0, 2, 1, 4).reshape(-1, P, BLK))

    x = np.concatenate([inp["x_prompt"].reshape(NP, D), inp["x_sample"].reshape(NB * NS, D)])
    a["xT"] = features(x)
    a["memT"] = features(inp["mem_prompt"][0])
    a["w_memk"] = col_tiles(inp["w_mem_k"][0])
    a["w_memv"] = c(inp["w_mem_v"][0].reshape(8, 2, P, 2, 512).transpose(3, 0, 2, 1, 4).reshape(-1, P, BLK))
    w_in = inp["w_in"][0]
    conv, gates0 = 2 * CC, w_in.shape[1] - 3 * D
    t = col_tiles(w_in[:, :gates0])
    ab = t[:2 * conv // P].reshape(2, CT, 2, P, BLK).transpose(1, 0, 2, 3, 4).reshape(-1, P, BLK)
    a["w_proj"] = c(np.concatenate([ab, t[2 * conv // P:]]))
    a["w_gate"] = col_tiles(w_in[:, gates0:])
    conv_o = inp["w_conv_o"][0].reshape(8, P, KT, P).transpose(2, 1, 0, 3).reshape(KT, P, BLK)
    mem_o = inp["w_mem_o"][0].reshape(8, P, KT, P).transpose(2, 1, 0, 3).reshape(KT, P, BLK)
    sw_o = inp["w_sw_o"][0].reshape(4, P, KT // 2, 2, P).transpose(2, 1, 3, 0, 4).reshape(KT // 2, P, BLK)
    a["w_oproj"] = c(np.stack([conv_o[0::2], mem_o[0::2], sw_o, conv_o[1::2], mem_o[1::2]], 1).reshape(-1, P, BLK))
    a["w_out"] = col_tiles(inp["w_out"][0])
    a["w_q"] = col_tiles(inp["peer_w_q"][0])
    u = inp["peer_u"][0].reshape(P, P, 2, 8, P)
    a["w_u"] = c(u.transpose(1, 2, 4, 3, 0).reshape(-1, P, BLK))
    v = inp["peer_v"][0].reshape(P, 8, 2, 8, KT, P)
    a["w_v"] = c(v.transpose(1, 4, 2, 0, 3, 5).reshape(-1, P, BLK))
    a["params"] = c(np.concatenate([
        vec(inp["norm1_g"][0]), vec(inp["mem_norm_g"][0]), vec(inp["norm2_g"][0]),
        inp["conv_w"][0].reshape(CW, CT, P).transpose(2, 1, 0).reshape(P, -1),
        vec(inp["conv_b"][0]), vec(inp["conv_ln_g"][0]), vec(inp["conv_ln_b"][0]),
        inp["sw_q_g"][0].T, inp["sw_k_g"][0].T, vec(inp["mem_q_g"][0]), vec(inp["mem_k_g"][0]),
        inp["peer_k1"][0].T, inp["peer_k2"][0].T], axis=1))
    a["conv_state"] = c(inp["state_conv"][0].reshape(NB, CW - 1, CT, P).transpose(3, 2, 0, 1))
    k_units, v_units = [], []
    for g, (w, r) in enumerate(zip(WINDOWS, DILATIONS)):
        kk, vv = inp[f"state_sw{g}_k"][0], inp[f"state_sw{g}_v"][0]
        a[f"sw{g}_k"], a[f"sw{g}_v"] = c(kk.reshape(NB, -1)), c(vv.reshape(NB, -1))
        for cls in range(min(r, NS)):
            k_units.append(kk[:, cls::r].transpose(0, 3, 2, 1).reshape(NB, P, HG * P))
            v_units.append(vv[:, cls::r].reshape(NB, P, HG * P))
    a["k_units"], a["v_units"] = c(np.stack(k_units, 1)), c(np.stack(v_units, 1))
    ck, cv = inp["cache_mem_k"][0], inp["cache_mem_v"][0]
    a["memk_c"] = c(ck.reshape(NB, NM, MH, 2, P).transpose(0, 4, 2, 3, 1).reshape(NB, P, -1))
    a["memv_c"] = c(cv.reshape(NB, 2, P, MH * MD).transpose(0, 2, 1, 3).reshape(NB, P, -1))
    a["ident"] = np.eye(P, dtype=np.float32)
    a["iota"] = c(np.broadcast_to(np.arange(P, dtype=np.float32), (P, P)))
    a["iota16"] = c(np.broadcast_to(np.arange(TOPK, dtype=np.float32), (P, TOPK)))
    sl = np.array(slopes(), np.float32)
    a["slope"] = c(np.broadcast_to(-sl, (P, G * HG)))
    t, s = np.arange(NP)[:, None], np.arange(NP)[None, :]
    dist = np.stack([np.where((s <= t) & ((t - s) % r == 0) & (t - s <= P * r), t - s, 1e30) for r in DILATIONS], 1)
    a["dist_p"] = c(dist.reshape(2, P, G, NP).transpose(1, 0, 2, 3).astype(np.float32))
    bias = np.full((HG, NS, SAMPLE_COLS), NEG, np.float32)
    for g, (w, r) in enumerate(zip(WINDOWS, DILATIONS)):
        for h in range(HG):
            for q in range(NS):
                for m in range(P):
                    d = w + q - (q % r + r * m)
                    if d <= P * r:
                        bias[h, q, g * P + m] = -sl[g * HG + h] * d
                for q2 in range(q % r, q + 1, r):
                    bias[h, q, G * P + g * NS + q2] = -sl[g * HG + h] * (q - q2)
    a["dist_s"] = c(np.broadcast_to(bias.reshape(1, 32, -1), (4, 32, SAMPLE_COLS)).reshape(P, -1))
    return a


def _outputs():
    o = {"y": (P, KT, NT), "convp": (P, CT, CW - 1), "convs": (P, CT, NB, CW - 1), "memk": (P, 2 * MH, NM),
         "memv": (2, P, MH * MD), "kp": (P, G * HG, NP), "vp": (P, 2, G * HG, P)}
    for g, w in enumerate(WINDOWS):
        o[f"sw{g}_k"] = o[f"sw{g}_v"] = (NB, w * HG * P)
    return o


def kernel(**inputs):
    import numpy as np
    import concourse.bacc as bacc
    from concourse.bass_utils import run_bass_kernel_spmd

    arrays = _lay_out({k: np.asarray(v) for k, v in inputs.items()})
    nc = bacc.Bacc("TRN2", target_bir_lowering=False, num_devices=1)
    a = {k: nc.dram_tensor("in_" + k, list(v.shape), F32, kind="ExternalInput").ap() for k, v in arrays.items()}
    o = {k: nc.dram_tensor("o_" + k, list(s), F32, kind="ExternalOutput").ap() for k, s in _outputs().items()}
    build(nc, a, o)
    r = run_bass_kernel_spmd(nc, [{"in_" + k: v for k, v in arrays.items()}], core_ids=[0]).results[0]
    r = {k: r["o_" + k] for k in o}

    y = r["y"].transpose(2, 1, 0).reshape(NT, D)
    kp = r["kp"].reshape(P, G, HG, NP).transpose(1, 3, 2, 0)
    vp = r["vp"].reshape(P, 2, G, HG, P).transpose(2, 1, 0, 3, 4).reshape(G, NP, HG, P)
    outs = [y[:NP].reshape(1, NP, D), y[NP:].reshape(NB, NS, D),
            r["convp"].transpose(2, 1, 0).reshape(1, 1, CW - 1, CC),
            r["convs"].transpose(2, 3, 1, 0).reshape(1, NB, CW - 1, CC)]
    for g, w in enumerate(WINDOWS):
        keep = min(w, NP)
        outs += [kp[g, NP - keep:].reshape(1, 1, keep, HG, P), vp[g, NP - keep:].reshape(1, 1, keep, HG, P)]
    for g, w in enumerate(WINDOWS):
        outs += [r[f"sw{g}_k"].reshape(1, NB, w, HG, P), r[f"sw{g}_v"].reshape(1, NB, w, HG, P)]
    outs += [r["memk"].reshape(P, MH, 2, NM).transpose(3, 1, 2, 0).reshape(1, 1, NM, MH, MD),
             r["memv"].reshape(1, 1, NM, MH, MD)]
    return tuple(np.ascontiguousarray(v) for v in outs)
```

```python
from contextlib import ExitStack

import concourse.bass as bass
from concourse import mybir

F32 = mybir.dt.float32
F32R = mybir.dt.float32r
U32 = mybir.dt.uint32
ALU = mybir.AluOpType
ACT = mybir.ActivationFunctionType
AX = mybir.AxisListType

P = 128
D = 2048
KT = D // P
NP, NB, NS = 256, 8, 8
NT = NP + NB * NS
CC, CW = 1024, 31
CT = CC // P
G, HG = 3, 4
WINDOWS, DILATIONS = (128, 512, 2048), (1, 4, 16)
UNITS = sum(min(r, NS) for r in DILATIONS)
NM, MH, MD = 256, 4, 256
PH, PK, TOPK = 8, 128, 16
EPS = 1e-6
BLK = 1024

MEMK_BLOCKS, MEMV_BLOCKS, PROJ_BLOCKS, GATE_BLOCKS = 16, 16, 120, 96
OPROJ_BLOCKS, OUT_BLOCKS, WQ_BLOCKS, U_BLOCKS, V_BLOCKS = 40, 32, 32, 256, 256
MEMK0 = 0
MEMV0 = MEMK0 + MEMK_BLOCKS
PROJ0 = MEMV0 + MEMV_BLOCKS
GATE0 = PROJ0 + PROJ_BLOCKS
OPROJ0 = GATE0 + GATE_BLOCKS
OUT0 = OPROJ0 + OPROJ_BLOCKS
WQ0 = OUT0 + OUT_BLOCKS
U0 = WQ0 + WQ_BLOCKS
V0 = U0 + U_BLOCKS
END = V0 + V_BLOCKS
MEMK_T, MEMV_T, PROJ_T, GATE_T = 0, 8, 12, 72
OUT_T, WQ_T, U_T, V_T = 120, 136, 152, 280

SELECT_TILES = 5
SPREAD_U = SELECT_TILES * PH
LAST_U = SPREAD_U + NT // 4
SAMPLE_COLS = G * P + G * 32
NORM_G, WIN_G, MEM_G, MEMS_G, WINS_G = 12, 2, 2, 6, 4
WIN_G0 = NORM_G
MEM_G0 = WIN_G0 + HG * WIN_G
MEMS_G0 = MEM_G0 + MH * MEM_G
WINS_G0 = MEMS_G0 + 2 * MEMS_G
KV_SLOTS = 8
NEG = -1.0e30


class Place:

    def __init__(self, const, *terms):
        self.const, self.terms = const, terms

    def __add__(self, k):
        return Place(self.const + k, *self.terms)

    def over(self, d):
        return Place(self.const // d, *[(per // d, reg) for per, reg in self.terms])

    def value(self, scale=1, plus=0):
        total = self.const * scale + plus
        for per, reg in self.terms:
            total = reg * (per * scale) + total
        return total


def slopes():
    n = G * HG
    return [2.0 ** (-8.0 * (i + 1) / n) for i in range(n)]


def build(nc, a, o):
    ctx = ExitStack()
    with ctx:
        def sb(name, shape, dt=F32, scope=ctx):
            return scope.enter_context(nc.sbuf_tensor(name, shape, dt))

        def sem(name):
            return ctx.enter_context(nc.semaphore(name))

        def scratch(name, shape):
            return nc.dram_tensor(name, shape, F32, kind="Internal").ap()

        raw = sb("raw", [P, 4, BLK])
        w_hi = sb("w_hi", [P, 4, BLK], F32R)
        w_lo = sb("w_lo", [P, 4, BLK], F32R)
        xs_hi = sb("xs_hi", [P, KT, NT], F32R)
        xs_lo = sb("xs_lo", [P, KT, NT], F32R)
        ident = sb("ident", [P, P])
        iota = sb("iota", [P, P])
        iota16 = sb("iota16", [P, TOPK])
        slope = sb("slope", [P, G * HG])
        ones = sb("ones", [P, P])
        prm = sb("prm", [P, a["params"].shape[1]])
        at = 0

        def param(n):
            nonlocal at
            at += n
            return prm[:, at - n:at]

        g1, gm, g2 = param(KT), param(KT), param(KT)
        cw, cb, lng, lnb = param(CT * CW), param(CT), param(CT), param(CT)
        qg, kg, mqg, mkg = param(G), param(G), param(2), param(2)
        k1T, k2T = param(PK), param(PK)

        low, high = ExitStack(), ExitStack()
        x_raw = sb("x_raw", [P, KT, NT], scope=low)
        m_raw = sb("m_raw", [P, KT, NM], scope=low)
        sq4 = sb("sq4", [P, 4, NT], scope=low)
        rms_x = sb("rms_x", [P, 2, NT], scope=low)
        low.close()
        low = ExitStack()
        hb = sb("hb", [P, 44, NT], scope=low)
        cc = sb("cc", [P, CT, NT], scope=low)
        gate_st = sb("gate_st", [P, 2, NT], scope=low)
        mk = sb("mk", [P, 2 * MH, NM], scope=high)
        mv = sb("mv", [P, 2, MH * MD], scope=high)
        rms_c = sb("rms_c", [P, 2, NT], scope=high)
        PW, SWD = NP + CW - 1, NS + CW - 1
        ex = ExitStack()
        ue = sb("ue", [P, CT, PW + NB * SWD], scope=ex)
        sig = sb("sig", [P, NT], scope=ex)
        ex.close()
        ex = ExitStack()
        qk_sq = sb("qk_sq", [P, HG, NT], scope=ex)
        qk_r = sb("qk_r", [P, HG, NT], scope=ex)
        r_row = sb("r_row", [HG, NT], scope=ex)
        to_row = sb("to_row", [P, HG, HG], scope=ex)
        from_row = sb("from_row", [HG, HG, P], scope=ex)
        ex.close()
        high.close()
        high = ExitStack()
        sS = sb("sS", [P, G * P + G * NP], scope=high)
        pT = sb("pT", [P, G * P + G * NP], scope=high)
        stat = sb("stat", [P, 8], scope=high)
        ex = ExitStack()
        vnp = sb("vnp", [P, 2, G * HG, P], scope=ex)
        nnew = sb("nnew", [NB * NS, 2, G * HG * P], scope=ex)
        dpr = sb("dpr", [P, 2, G, NP], scope=ex)
        q_st = sb("q_st", [P, G, NP], scope=ex)
        v_st = sb("v_st", [P, 2, G, P], scope=ex)
        ex.close()
        ex = ExitStack()
        km = sb("km", [P, 2, 2 * MH * NM], scope=ex)
        mq_st = sb("mq_st", [P, 2, NP], scope=ex)
        mv_st = sb("mv_st", [P, 2, MD], scope=ex)
        zm = sb("zm", [P, 2, MH, 32], scope=ex)
        ex.close()
        high.close()
        high = ExitStack()
        kv = sb("kv", [P, KV_SLOTS, HG * P], scope=high)
        vnew = sb("vnew", [4 * NS, G * HG * P], scope=high)
        z = sb("z", [P, UNITS, HG, 32], scope=high)
        z4 = sb("z4", [P, G, HG, P], scope=high)
        dsm = sb("dsm", [P, SAMPLE_COLS], scope=high)
        sT = sb("sT", [P, SAMPLE_COLS], scope=high)
        pTs = sb("pTs", [P, G * P], scope=high)
        pTn = sb("pTn", [4 * NS, G * P], scope=high)
        osb = sb("osb", [P, P], scope=high)
        stat2 = sb("stat2", [P, 8], scope=high)
        high.close()
        high = ExitStack()
        osw_hi = sb("osw_hi", [P, HG, NT], F32R, scope=high)
        osw_lo = sb("osw_lo", [P, HG, NT], F32R, scope=high)
        gl = sb("gl", [P, 2, 3, NT], scope=high)
        mt = sb("mt", [P, 4, NT], scope=high)
        high.close()
        low.close()
        low = ExitStack()
        xs2_hi = sb("xs2_hi", [P, KT, NT], F32R, scope=low)
        xs2_lo = sb("xs2_lo", [P, KT, NT], F32R, scope=low)
        acc = sb("acc", [P, KT, NT], scope=low)
        gelu_st = sb("gelu_st", [P, 2, NT], scope=low)
        T = sb("T", [P, 3, NT], scope=low)
        ph = ExitStack()
        qT = sb("qT", [P, 2 * PH, NT], scope=ph)
        ex = ExitStack()
        sqh = sb("sqh", [P, 4, NT], scope=ex)
        rms_h = sb("rms_h", [P, 2, NT], scope=ex)
        ex.close()
        pq_st = sb("pq_st", [P, 2, NT], scope=ph)
        tS = sb("tS", [P, 6 * PK], scope=ph)
        tW = sb("tW", [P, 6 * PK], scope=ph)
        eq = sb("eq", [P, 3, TOPK, TOPK], scope=ph)
        tv = sb("tv", [P, 6, TOPK], scope=ph)
        tiu = sb("tiu", [P, 6, TOPK], U32, scope=ph)
        tif = sb("tif", [P, 6, TOPK], scope=ph)
        cv = sb("cv", [P, 3, TOPK], scope=ph)
        ci = sb("ci", [P, 3, TOPK], U32, scope=ph)
        cab = sb("cab", [P, 2, 3, TOPK], U32, scope=ph)
        cabf = sb("cabf", [P, 2, 3, TOPK], scope=ph)
        ce = sb("ce", [P, 3, TOPK], scope=ph)
        tz = sb("tz", [P, 12], scope=ph)
        R = sb("R", [P, 3, 3, PH, TOPK], scope=ph)
        ph.close()
        ph = ExitStack()
        hot = sb("hot", [P, 2, 4, 2, PK], scope=ph)
        gd = sb("gd", [P, 2, PK, 32], scope=ph)
        ph.close()
        ph = ExitStack()
        actc = sb("actc", [P, 2, 4, NT], scope=ph)
        gc = sb("gc", [P, 2, NT // 32, 4, 32], scope=ph)
        cf = sb("cf", [P, 2, 2, NT], scope=ph)
        ph.close()
        low.close()

        ps = ctx.enter_context(nc.psum_tensor("ps", [P, 8, 512], F32))

        gates_d = scratch("gates_d", [3 * KT, P, NT])
        new_d = scratch("new_d", [2, NB * NS, G * HG * P])
        act_d = scratch("act_d", [P, P, NT])
        gd_d = scratch("gd_d", [NT // 32, P, PK * 32])

        m_loaded, x_loaded, const_loaded = sem("m_loaded"), sem("x_loaded"), sem("const_loaded")
        raw_loaded = [sem(f"raw_loaded{i}") for i in range(4)]
        hi_done, lo_done, w_released = sem("hi_done"), sem("lo_done"), sem("w_released")
        bank_free = sem("bank_free")
        sq_done, sq_summed, rooted, normed = sem("sq_done"), sem("sq_summed"), sem("rooted"), sem("normed")
        xs_hi_done, xs_lo_done = sem("xs_hi_done"), sem("xs_lo_done")
        x_hi_half, x_lo_half = sem("x_hi_half"), sem("x_lo_half")
        dve_set = sem("dve_set")
        state_copied, conv_prev_loaded = sem("state_copied"), sem("conv_prev_loaded")
        sig_done = sem("sig_done")
        gates_stored = [sem("gates_stored0"), sem("gates_stored1")]
        conv_done, ln_summed, ln_centered = sem("conv_done"), sem("ln_summed"), sem("ln_centered")
        ln_squared, ln_rooted, ln_scaled = sem("ln_squared"), sem("ln_rooted"), sem("ln_scaled")
        mk_ready, row_ready, row_spread = sem("mk_ready"), sem("row_ready"), sem("row_spread")
        conv_stored, mem_stored, kp_stored, vp_stored = (
            sem("conv_stored"), sem("mem_stored"), sem("kp_stored"), sem("vp_stored"))
        vt_turned, vt_copied, new_stored, tails_copied = (
            sem("vt_turned"), sem("vt_copied"), sem("new_stored"), sem("tails_copied"))
        dist_p_loaded, dist_s_loaded = sem("dist_p_loaded"), sem("dist_s_loaded")
        a_staged, a_scored, a_biased, a_exped = sem("a_staged"), sem("a_scored"), sem("a_biased"), sem("a_exped")
        a_probs, a_turned, a_copied, a_mixed, a_kept = (
            sem("a_probs"), sem("a_turned"), sem("a_copied"), sem("a_mixed"), sem("a_kept"))
        m_staged, m_scored, m_maxed, m_exped, m_probs = (
            sem("m_staged"), sem("m_scored"), sem("m_maxed"), sem("m_exped"), sem("m_probs"))
        m_turned, m_copied, m_mixed, m_kept = sem("m_turned"), sem("m_copied"), sem("m_mixed"), sem("m_kept")
        km_loaded, km_prompt_loaded = [sem("km_loaded0"), sem("km_loaded1")], sem("km_prompt_loaded")
        zm_set, zm_used = sem("zm_set"), sem("zm_used")
        n_maxed, n_exped, n_probs, n_turned = sem("n_maxed"), sem("n_exped"), sem("n_probs"), sem("n_turned")
        n_copied, n_out, n_back, n_kept = sem("n_copied"), sem("n_out"), sem("n_back"), sem("n_kept")
        kv_loaded = [sem(f"kv_loaded{i}") for i in range(KV_SLOTS)]
        kv_used, z_set, z_used, vnew_loaded = sem("kv_used"), sem("z_set"), sem("z_used"), sem("vnew_loaded")
        s_maxed, s_exped, s_probs, s_turned = sem("s_maxed"), sem("s_exped"), sem("s_probs"), sem("s_turned")
        s_copied, s_out, s_back, s_kept = sem("s_copied"), sem("s_out"), sem("s_back"), sem("s_kept")
        osw_hi_done, osw_lo_done = sem("osw_hi_done"), sem("osw_lo_done")
        gl_loaded, o_taken = [sem("gl_loaded0"), sem("gl_loaded1")], sem("o_taken")
        merged, merged_hi, merged_lo, acc_loaded = sem("merged"), sem("merged_hi"), sem("merged_lo"), sem("acc_loaded")
        act_stored = [sem("act_stored0"), sem("act_stored1")]
        t_staged, t_scored, t_picked, t_exped, r_done = (
            sem("t_staged"), sem("t_scored"), sem("t_picked"), sem("t_exped"), sem("r_done"))
        r_turned, t_set, hot_set, hot_used, g_spread = (
            sem("r_turned"), sem("t_set"), sem("hot_set"), sem("hot_used"), sem("g_spread"))
        gd_stored = [sem("gd_stored0"), sem("gd_stored1")]
        chunk_loaded = [sem("chunk_loaded0"), sem("chunk_loaded1")]
        c_made, c_hi, c_lo = sem("c_made"), sem("c_hi"), sem("c_lo")
        y_stored = sem("y_stored")

        def taken(t):
            return t + 3

        def tile_view(t, i, lo=0, n=NT):
            return t[:, bass.ds(i, 1), lo:lo + n].rearrange("p o n -> p (o n)")

        def strided(view, offset, dims):
            return bass.AP(view.tensor, view.offset + offset, [list(view.ap[0])] + dims)

        DIAG = 32 + NS
        ZU = HG * 32

        def z_views(zt, src_of):
            zz = zt[:, :, :, :]
            return [
                (strided(zz, 0, [[DIAG, HG], [1, NS]]), src_of(0)),
                (strided(zz, ZU, [[ZU + 1, 4], [DIAG, HG], [4, 2]]),
                 src_of(1).rearrange("p h (i c) -> p c h i", c=4)),
                (strided(zz, 5 * ZU, [[ZU + 1, NS], [DIAG, HG]]), src_of(2).rearrange("p h t -> p t h")),
            ]

        block = ctx.enter_context(nc.Block())

        @block.sync
        def _(sp):
            def load(src, i, n):
                if n.const >= 4 or n.terms:
                    sp.wait_ge(lo_done, n.value(plus=-3))
                sp.dma_start(raw[:, n.const % 4, :],
                             src[bass.ds(i, 1)].rearrange("o p n -> (o p) n")).then_inc(raw_loaded[n.const % 4], 16)

            def rest_of_stage(src, base, blocks):
                with sp.Fori(1, blocks // 4) as i:
                    for r in range(4):
                        load(src, i * 4 + r, Place(base + r, (4, i)))

            def first_of_stage(src, base):
                for r in range(4):
                    load(src, r, Place(base + r))

            sp.dma_start(m_raw[:], a["memT"]).then_inc(m_loaded, 16)
            sp.dma_start(x_raw[:], a["xT"]).then_inc(x_loaded, 16)
            for name, base, blocks in (("w_memk", MEMK0, MEMK_BLOCKS), ("w_memv", MEMV0, MEMV_BLOCKS),
                                       ("w_proj", PROJ0, PROJ_BLOCKS)):
                first_of_stage(a[name], base)
                rest_of_stage(a[name], base, blocks)
            gates = a["w_gate_oproj"]
            first_of_stage(gates, GATE0)
            rest_of_stage(gates, GATE0, 2 * MEMS_G0 + 4)

            def two_tiles_ahead(tile, per, i):
                for r in range(4):
                    k = 2 * tile + 4 + r
                    load(gates, i * (2 * per) + k, Place(GATE0 + k, (2 * per, i)))

            sp.wait_ge(m_kept, MH)
            with sp.Fori(0, 2) as i:
                for part in range(2):
                    for bq in range(4):
                        if bq == 2:
                            two_tiles_ahead(MEMS_G0 + 2 * part, MEMS_G, i)
                        sp.wait_ge(zm_used, i * 8 + (part * 4 + bq + 1))
                        sp.dma_start(km[:, bq % 2, :], (a["memv_c"] if part else a["memk_c"])[
                            bass.ds(i * 4 + bq, 1)].rearrange("o p n -> (o p) n")).then_inc(km_loaded[bq % 2], 16)
                two_tiles_ahead(MEMS_G0 + 4, MEMS_G, i)
            sp.wait_ge(n_kept, 2)
            with sp.Fori(0, 2) as i:
                for part, name in enumerate(("k_units", "v_units")):
                    two_tiles_ahead(WINS_G0 + 2 * part, WINS_G, i)
                    units = a[name].rearrange("b u p n -> (b u) p n")

                    def unit(j, m):
                        slot = (part * 4 * UNITS + m) % KV_SLOTS
                        sp.wait_ge(kv_used, i * (8 * UNITS) + j * KV_SLOTS + (part * 4 * UNITS + m + 1))
                        sp.dma_start(kv[:, slot, :], units[bass.ds(i * (4 * UNITS) + j * KV_SLOTS + m, 1)].rearrange(
                            "o p n -> (o p) n")).then_inc(kv_loaded[slot], 16)

                    rest = 4 * UNITS % KV_SLOTS
                    if part:
                        for m in range(rest):
                            unit(0, m)
                    with sp.Fori(0, 4 * UNITS // KV_SLOTS) as j:
                        for m in range(KV_SLOTS):
                            unit(j, m + rest * part)
                    if not part:
                        for m in range(4 * UNITS - rest, 4 * UNITS):
                            unit(0, m)
            with sp.Fori(1, OPROJ_BLOCKS // 4) as i:
                for r in range(4):
                    load(gates, i * 4 + (GATE_BLOCKS + r), Place(OPROJ0 + r, (4, i)))
            for name, base, blocks in (("w_out", OUT0, OUT_BLOCKS), ("w_q", WQ0, WQ_BLOCKS),
                                       ("w_u", U0, U_BLOCKS), ("w_v", V0, V_BLOCKS)):
                first_of_stage(a[name], base)
                rest_of_stage(a[name], base, blocks)
            sp.wait_ge(bank_free, taken(V_T + V_BLOCKS // 2 - 1))
            sp.dma_start(o["y"], acc[:]).then_inc(y_stored, 16)
            for s, n in ((y_stored, 1), (conv_stored, 1 + CT), (mem_stored, 2), (kp_stored, G), (vp_stored, 1),
                         (state_copied, 2 * NB * (2 + 4)), (tails_copied, 2 * G)):
                sp.wait_ge(s, 16 * n)

        @block.gpsimd
        def _(pool):
            for dst, name in ((ident, "ident"), (iota, "iota"), (iota16, "iota16"), (slope, "slope"), (prm, "params")):
                pool.dma_start(dst[:], a[name]).then_inc(const_loaded, 16)
            for ct in range(CT):
                pool.dma_start(ue[:, ct, PW:].rearrange("p (b w) -> p b w", b=NB)[:, :, 0:CW - 1],
                               a["conv_state"][:, ct]).then_inc(conv_prev_loaded, 16)

            def keep(g, name, b, part, parts):
                batch, n = WINDOWS[g] * HG * P, (WINDOWS[g] - NS) * HG * P // parts
                at = b * batch + part * n
                src = a[f"sw{g}_{name}"].rearrange("b n -> (b n)")[bass.ds(at + NS * HG * P, n)]
                dst = o[f"sw{g}_{name}"].rearrange("b n -> (b n)")[bass.ds(at, n)]
                pool.dma_start(dst.rearrange("(c n) -> c n", c=16), src.rearrange("(c n) -> c n", c=16)
                               ).then_inc(state_copied, 16)

            def keep_state(name, tile, tiles):
                with pool.Fori(0, NB) as b:
                    pool.wait_ge(bank_free, b * tiles + taken(tile))
                    keep(0, name, b, 0, 1)
                    keep(1, name, b, 0, 1)
                    with pool.Fori(0, 4) as part:
                        pool.wait_ge(bank_free, b * tiles + part + taken(tile + 1))
                        keep(2, name, b, part, 4)

            keep_state("k", PROJ_T, 6)
            pool.wait_ge(bank_free, taken(PROJ_T + 2 * CT - 1))
            pool.dma_start(o["convp"], ue[:, :, NP:PW]).then_inc(conv_stored, 16)
            for ct in range(CT):
                pool.dma_start(o["convs"][:, ct], ue[:, ct, PW:].rearrange("p (b w) -> p b w", b=NB)[:, :, NS:SWD]
                               ).then_inc(conv_stored, 16)
            pool.wait_ge(mk_ready, 1)
            pool.dma_start(o["memk"], mk[:]).then_inc(mem_stored, 16)
            pool.dma_start(o["memv"].rearrange("s p n -> p s n"), mv[:]).then_inc(mem_stored, 16)
            pool.wait_ge(mem_stored, 16 * 2)
            pool.wait_ge(conv_stored, 16 * (1 + CT))
            pool.wait_ge(normed, 4 + 2 * G)
            pool.dma_start(dpr[:], a["dist_p"]).then_inc(dist_p_loaded, 16)
            for g in range(G):
                pool.dma_start(o["kp"][:, g * HG:(g + 1) * HG, :], hb[:, g * 12 + 4:g * 12 + 8, 0:NP]).then_inc(
                    kp_stored, 16)
            pool.wait_ge(vt_copied, 4 * G)
            pool.dma_start(o["vp"], vnp[:]).then_inc(vp_stored, 16)
            for part in range(2):
                pool.dma_start(new_d[part], nnew[:, part, :]).then_inc(new_stored, 16)
            pool.wait_ge(new_stored, 16 * 2)
            for g in range(G):
                for part, name in enumerate("kv"):
                    src = new_d[part].rearrange("(b t) c -> b t c", b=NB)[:, :, g * HG * P:(g + 1) * HG * P]
                    dst = o[f"sw{g}_{name}"].rearrange("b (l c) -> b l c", c=HG * P)[:, WINDOWS[g] - NS:, :]
                    pool.dma_start(dst, src).then_inc(tails_copied, 16)
            pool.wait_ge(vp_stored, 16)
            pool.wait_ge(a_kept, HG)
            pool.dma_start(km[:, 0, :], o["memk"].rearrange("p t n -> p (t n)")).then_inc(km_prompt_loaded, 16)
            pool.dma_start(km[:, 1, :].rearrange("p (s n) -> p s n", s=2),
                           o["memv"].rearrange("s p n -> p s n")).then_inc(km_prompt_loaded, 16)
            pool.wait_ge(n_kept, 2)
            pool.dma_start(dsm[:], a["dist_s"]).then_inc(dist_s_loaded, 16)
            for i in range(2):
                pool.wait_ge(z_used, 10 * i + 1)
                pool.dma_start(vnew[:], new_d[1, 32 * i:32 * i + 32, :]).then_inc(vnew_loaded, 16)
            pool.wait_ge(s_kept, 2)
            for s in gates_stored:
                pool.wait_ge(s, 16 * (3 * KT // 2))
            by_tile = gates_d.rearrange("(b m) p n -> m p b n", b=3)
            with pool.Fori(0, KT // 2) as i:
                for r in range(2):
                    pool.wait_ge(o_taken, i * 2 + (r + 1))
                    pool.dma_start(gl[:, r], by_tile[bass.ds(i * 2 + r, 1)].rearrange("o p b n -> (o p) b n")
                                   ).then_inc(gl_loaded[r], 16)
            pool.wait_ge(w_released, OUT0)
            pool.wait_ge(o_taken, KT + 2)
            pool.dma_start(acc[:], a["xT"]).then_inc(acc_loaded, 16)

            def load_chunk(q, c):
                pool.dma_start(actc[:, c], act_d[bass.ds(q * 4, 4)].rearrange("i p n -> p i n")
                               ).then_inc(chunk_loaded[c], 16)
                pool.dma_start(gc[:, c].rearrange("p b i t -> p b (i t)"),
                               gd_d[:, :, bass.ds(q * 128, 128)].rearrange("b p n -> p b n")
                               ).then_inc(chunk_loaded[c], 16)

            keep_state("v", OUT_T, 9)
            with pool.Fori(0, NT // 64) as tb:
                for s in range(2):
                    pool.wait_ge(g_spread, tb * 16 + (2 + (s + 1) * 8))
                    pool.dma_start(gd_d[bass.ds(tb * 2 + s, 1)].rearrange("o p n -> (o p) n"),
                                   gd[:, s].rearrange("p i t -> p (i t)")).then_inc(gd_stored[s], 16)
            for s in range(2):
                pool.wait_ge(gd_stored[s], 16 * (NT // 64))
            for s in act_stored:
                pool.wait_ge(s, 16 * (LAST_U // 2))
            load_chunk(0, 0)
            load_chunk(1, 1)
            for q in range(4):
                pool.wait_ge(c_made, 2 * q + 2)
                load_chunk(q + 2, q % 2)
            for s in act_stored:
                pool.wait_ge(s, 16 * (P // 2))
            with pool.Fori(3, 16) as i:
                for c in range(2):
                    pool.wait_ge(c_made, i * 4 + (2 * c - 2))
                    load_chunk(i * 2 + c, c)

        @block.scalar
        def _(act):
            A = act.activation

            def split_hi(n):
                s = n.const % 4
                act.wait_ge(raw_loaded[s], n.over(4).value(16, 16))
                if n.const >= 4 or n.terms:
                    act.wait_ge(w_released, n.value(plus=-3))
                A(w_hi[:, s, :], raw[:, s, :], ACT.Copy).then_inc(hi_done, 1)

            def width_norm(src, cols, k, sq, root, bank):
                for c in range(4):
                    if c:
                        act.wait_ge(sq_summed, 4 * k + c)
                    A(sq[:, :, 0:cols], src[:, 4 * c:4 * c + 4, :], ACT.Square).then_inc(sq_done, 1)
                act.wait_ge(sq_summed, 4 * k + 4)
                A(root[:, 0, 0:cols], ps[:, bank, 0:cols], ACT.Sqrt, bias=EPS, scale=1.0 / D).then_inc(rooted, 1)

            act.sem_inc(g_spread, 2)
            act.wait_ge(m_loaded, 16)
            width_norm(m_raw, NM, 0, sq4, rms_x, 2)
            act.wait_ge(normed, 1)
            A(xs_hi[:, :, 0:NM], m_raw[:], ACT.Copy).then_inc(xs_hi_done, 1)
            for n in range(4):
                split_hi(Place(n))
            act.wait_ge(x_loaded, 16)
            width_norm(x_raw, NT, 1, sq4, rms_x, 3)
            with act.Fori(0, (MEMK_BLOCKS + MEMV_BLOCKS) // 4) as i:
                for r in range(4):
                    split_hi(Place(4 + r, (4, i)))
            act.wait_ge(w_released, PROJ0)
            act.wait_ge(normed, 2)
            A(xs_hi[:, 0:8, :], x_raw[:, 0:8, :], ACT.Copy).then_inc(x_hi_half, 1)
            A(xs_hi[:, 8:16, :], x_raw[:, 8:16, :], ACT.Copy).then_inc(xs_hi_done, 1)
            with act.Fori(0, CT // 2) as i:
                for u in range(2):
                    n = Place(PROJ0 + 4 * u, (8, i))
                    for r in range(4):
                        split_hi(n + (r + 4))
                    act.wait_ge(bank_free, i * 4 + taken(PROJ_T + 2 * u - 1))
                    A(sig[:], ps[:, 2 * u + 1, 0:NT], ACT.Sigmoid).then_inc(sig_done, 1)
            with act.Fori(0, 22) as i:
                n = Place(PROJ0 + 4 * CT, (4, i))
                for j in range(2):
                    split_hi(n + (2 * j + 4))
                    split_hi(n + (2 * j + 5))
                    act.copy(tile_view(hb, i * 2 + j), ps[:, j, 0:NT]).then_inc(bank_free, 1)

            def gate(t, per=0, i=None):
                n = Place(GATE0 + 2 * t, *([(2 * per, i)] if per else []))
                split_hi(n + 4)
                split_hi(n + 5)
                if t >= 2:
                    act.wait_ge(gates_stored[t % 2], (i * (8 * per) if per else 0) + 16 * (t // 2))
                A(gate_st[:, t % 2, :], ps[:, t % 2, 0:NT], ACT.Sigmoid).then_inc(bank_free, 1)
                if per:
                    act.wait_ge(bank_free, i * per + taken(GATE_T + t))
                    dst = gates_d[bass.ds(i * per + t, 1)].rearrange("o p n -> (o p) n")
                else:
                    act.wait_ge(bank_free, taken(GATE_T + t))
                    dst = gates_d[t]
                act.dma_start(dst, gate_st[:, t % 2, :]).then_inc(gates_stored[t % 2], 16)

            act.wait_ge(conv_stored, 16 * (1 + CT))
            act.wait_ge(ln_centered, 1)
            for c in range(2):
                if c:
                    act.wait_ge(ln_summed, 2)
                A(qk_sq[:], cc[:, 4 * c:4 * c + 4, :], ACT.Square).then_inc(ln_squared, 1)
            gate(0)
            act.wait_ge(ln_summed, 3)
            A(rms_c[:, 0, :], ps[:, 3, 0:NT], ACT.Sqrt, bias=EPS, scale=1.0 / CC).then_inc(ln_rooted, 1)
            for c in range(2):
                act.wait_ge(ln_summed, 3 + c)
                A(qk_sq[:, :, 0:NM], mk[:, 4 * c:4 * c + 4, :], ACT.Square).then_inc(ln_squared, 1)
            gate(1)
            act.wait_ge(ln_summed, 5)
            A(qk_r[:, :, 0:NM].rearrange("p (b h) n -> p b h n", b=2),
              ps[:, 4:6, :].rearrange("p b (h n) -> p b h n", h=2), ACT.Sqrt, bias=EPS, scale=1.0 / MD
              ).then_inc(ln_rooted, 1)
            def squares(k):
                first = (k // 2) * 12 + (k % 2) * HG if k < 2 * G else 36 + (k - 2 * G) * HG
                A(qk_sq[:], hb[:, first:first + HG, :], ACT.Square).then_inc(sq_done, 1)

            def root(k):
                act.wait_ge(sq_summed, 8 + k + 1)
                if k >= 2 * G:
                    A(r_row[0:2, :], ps[0:2, 2, 0:NT], ACT.Sqrt, bias=MD * EPS).then_inc(rooted, 1)
                elif k % 2:
                    A(r_row[:], ps[0:HG, 2, 0:NT], ACT.Sqrt, bias=EPS, scale=1.0 / P).then_inc(rooted, 1)
                else:
                    A(r_row[:], ps[0:HG, 2, 0:NT], ACT.Sqrt, bias=P * EPS).then_inc(rooted, 1)

            squares(0)
            root(0)
            for k in range(2 * G + 2):
                if k < 2 * G + 1:
                    squares(k + 1)
                gate(2 + k)
                if k < 2 * G + 1:
                    root(k + 1)
            gate(10)
            act.wait_ge(ln_scaled, 1)
            for ct in range(CT):
                A(cc[:, ct, :], cc[:, ct, :], ACT.Silu, bias=lnb[:, ct:ct + 1], scale=lng[:, ct:ct + 1])
            gate(11)
            act.drain()

            S0, S1 = slice(0, G * P), slice(G * P, G * (P + NP))
            with act.Fori(0, HG) as h:
                act.wait_ge(a_biased, h + 1)
                for qb, cols in enumerate((S0, S1)):
                    e = A(sS[:, cols], sS[:, cols], ACT.Exp, bias=stat[:, qb:qb + 1], accum_out=stat[:, 2 + qb:3 + qb])
                e.then_inc(a_exped, 1)
                gate(WIN_G0, WIN_G, h)
                act.wait_ge(a_turned, h + 1)
                act.copy(pT[:, 0:3 * P], ps[:, 5, 0:3 * P])
                act.copy(pT[:, 3 * P:9 * P], ps[:, 6:8, 0:3 * P]).then_inc(a_copied, 1)
                gate(WIN_G0 + 1, WIN_G, h)

            with act.Fori(0, MH) as h:
                act.wait_ge(m_maxed, h + 1)
                for qb in range(2):
                    e = A(sS[:, qb * NM:(qb + 1) * NM], ps[:, 2, qb * NM:(qb + 1) * NM], ACT.Exp,
                          bias=stat[:, qb:qb + 1], accum_out=stat[:, 2 + qb:3 + qb])
                e.then_inc(m_exped, 1)
                gate(MEM_G0, MEM_G, h)
                act.wait_ge(m_turned, h + 1)
                act.copy(pT[:, 0:2 * NP], ps[:, 3, :]).then_inc(m_copied, 1)
                gate(MEM_G0 + 1, MEM_G, h)
            with act.Fori(0, 2) as i:
                gate(MEMS_G0, MEMS_G, i)
                act.wait_ge(n_maxed, i + 1)
                A(sS[:, 0:NM], ps[:, 2, 0:NM], ACT.Exp, bias=stat[:, 0:1],
                  accum_out=stat[:, 2:3]).then_inc(n_exped, 1)
                gate(MEMS_G0 + 1, MEMS_G, i)
                act.wait_ge(n_turned, i + 1)
                act.copy(pT[:, 0:NM], ps[:, 3, 0:NM]).then_inc(n_copied, 1)
                gate(MEMS_G0 + 2, MEMS_G, i)
                gate(MEMS_G0 + 3, MEMS_G, i)
                act.wait_ge(zm_used, i * 8 + 10)
                act.copy(sS[:, NM:2 * NM], ps[:, 4, 0:MD]).then_inc(n_out, 1)
                gate(MEMS_G0 + 4, MEMS_G, i)
                gate(MEMS_G0 + 5, MEMS_G, i)
            with act.Fori(0, 2) as i:
                gate(WINS_G0, WINS_G, i)
                act.wait_ge(s_maxed, i + 1)
                A(sT[:], sT[:], ACT.Exp, bias=stat2[:, 0:1], accum_out=stat2[:, 1:2]).then_inc(s_exped, 1)
                gate(WINS_G0 + 1, WINS_G, i)
                act.wait_ge(s_turned, i + 1)
                act.copy(pTs[:], ps[:, 3, 0:G * P])
                act.copy(pTn[:], ps[0:4 * NS, 4, 0:G * P]).then_inc(s_copied, 1)
                gate(WINS_G0 + 2, WINS_G, i)
                gate(WINS_G0 + 3, WINS_G, i)

            act.wait_ge(w_released, OPROJ0)
            A(xs_hi[:, 0:CT, :], cc[:], ACT.Copy).then_inc(xs_hi_done, 1)
            act.wait_ge(s_kept, 2)
            A(xs_hi[:, CT:2 * CT, :], hb[:, 36:44, :], ACT.Copy).then_inc(xs_hi_done, 1)
            A(osw_hi[:], hb[:, 8:8 + HG, :], ACT.Copy).then_inc(osw_hi_done, 1)
            with act.Fori(0, 2) as i:
                n = Place(OPROJ0, (20, i))
                for m in range(KT // 2):
                    for r in range(3 if m % 2 == 0 else 2):
                        split_hi(n + ((m // 2) * 5 + (0 if m % 2 == 0 else 3) + r + 4))
                    act.wait_ge(merged, i * 8 + (m + 1))
                    A(tile_view(xs2_hi, i * 8 + m), mt[:, 3, :], ACT.Copy).then_inc(merged_hi, 1)
            with act.Fori(0, OUT_BLOCKS // 4) as i:
                for r in range(4):
                    split_hi(Place(OUT0 + 4 + r, (4, i)))
                act.wait_ge(bank_free, i * 2 + taken(OUT_T + 1))
                act.wait_ge(sq_summed, i + 16)
                A(sqh[:, 0:2, :], acc[:, bass.ds(i * 2, 2), :], ACT.Square).then_inc(sq_done, 1)
            act.wait_ge(sq_summed, 24)
            A(rms_h[:, 0, :], ps[:, 2, 0:NT], ACT.Sqrt, bias=EPS, scale=1.0 / D).then_inc(rooted, 1)
            for c in range(4):
                act.wait_ge(normed, 11 + c)
                A(xs_hi[:, 4 * c:4 * c + 4, :], qT[:, 4 * c:4 * c + 4, :], ACT.Copy).then_inc(xs_hi_done, 1)
            with act.Fori(0, WQ_BLOCKS // 4) as i:
                for j in range(2):
                    n = Place(WQ0, (4, i))
                    split_hi(n + (2 * j + 4))
                    split_hi(n + (2 * j + 5))
                    act.copy(tile_view(qT, i * 2 + j), ps[:, j, 0:NT]).then_inc(bank_free, 1)

            def gelu(n, j, stored, before=None):
                split_hi(n + 4)
                if before:
                    before()
                split_hi(n + 5)
                if stored is not None:
                    act.wait_ge(act_stored[j % 2], stored)
                A(gelu_st[:, j % 2, :], ps[:, j % 2, 0:NT], ACT.Gelu_apprx_tanh).then_inc(bank_free, 1)
                tile = n.over(2) + (U_T - U0 // 2)
                act.wait_ge(bank_free, tile.value(plus=3))
                if n.terms:
                    dst = act_d[bass.ds((tile + -U_T).value(), 1)].rearrange("o p n -> (o p) n")
                else:
                    dst = act_d[tile.const - U_T]
                act.dma_start(dst, gelu_st[:, j % 2, :]).then_inc(act_stored[j % 2], 16)

            def top_gates(heads):
                act.wait_ge(t_picked, heads)
                for tt in range(3):
                    e = A(ce[:, tt, :], cv[:, tt, :], ACT.Exp, bias=tz[:, tt:tt + 1],
                          accum_out=tz[:, 3 + tt:4 + tt])
                e.then_inc(t_exped, 1)

            def select(h2):
                for j in range(2 * SELECT_TILES):
                    if h2 is None:
                        gelu(Place(U0 + 2 * j), j, 16 * (j // 2) if j >= 2 else None)
                    else:
                        gelu(Place(U0 + 2 * j, (20, h2)), j, h2 * 80 + 16 * (j // 2))
                    if j % SELECT_TILES == SELECT_TILES - 2:
                        u = j // SELECT_TILES
                        top_gates(u + 1 if h2 is None else h2 * 2 + (u + 1))

            select(None)
            with act.Fori(1, PH // 2) as h2:
                select(h2)

            def spread(tb, first):
                for m in range(16):
                    k = SPREAD_U + m
                    gelu(Place(U0 + 2 * k, (32, tb)), m, tb * 128 + 16 * (k // 2))
                    if not first and m % 8 == 0:
                        act.wait_ge(gd_stored[m // 8], tb * 16)
                    act.wait_ge(hot_used, tb * 16 + (m + 3))
                    out = strided(gd[:, m // 8, :, :], 4 * (m % 8), [[1, 4], [32, PK]])
                    act.copy(out, ps[:, 2 + m % 2, :].rearrange("p (t i) -> p t i", t=4)).then_inc(g_spread, 1)

            spread(0, True)
            with act.Fori(1, NT // 64) as tb:
                spread(tb, False)

            def c_split(step, dst):
                act.wait_ge(c_made, step.value(plus=1))
                A(dst, cf[:, step.const % 2], ACT.Copy).then_inc(c_hi, 1)

            for p in range(8):
                k = LAST_U + p
                gelu(Place(U0 + 2 * k), k, 16 * (k // 2), lambda: c_split(Place(p), xs2_hi[:, 2 * p:2 * p + 2, :]))

            def v_group(gg, group, dst):
                with act.Fori(0, 2) as i:
                    for p in range(4):
                        n = Place(V0 + group * 32 + 4 * p, (16, i), *([(64, gg)] if gg is not None else []))
                        for r in range(4):
                            split_hi(n + (4 + r))
                            if r == 0:
                                step = Place(8 + group * 8 + p, (4, i), *([(16, gg)] if gg is not None else []))
                                c_split(step, dst[:, bass.ds(i * 8 + 2 * p, 2), :])

            with act.Fori(0, 3) as gg:
                v_group(gg, 0, xs_hi)
                v_group(gg, 1, xs2_hi)
            v_group(None, 6, xs_hi)
            with act.Fori(0, 7) as i:
                for r in range(4):
                    split_hi(Place(V0 + 7 * 32 + 4 + r, (4, i)))

        @block.vector
        def _(dve):
            TT, STT, TS = dve.tensor_tensor, dve.scalar_tensor_tensor, dve.tensor_scalar

            def move(out, src):
                return TS(out, src, 1.0, None, ALU.mult)

            def split_lo(n):
                s = n.const % 4
                dve.wait_ge(hi_done, n.value(plus=1))
                TT(w_lo[:, s, :], raw[:, s, :], w_hi[:, s, :].bitcast(F32), ALU.subtract).then_inc(lo_done, 1)

            def ended(n):
                dve.wait_ge(w_released, n.value(plus=1))

            def scale_by_norm(dst, src, gain, root, cols, first, tiles):
                for k in range(first, first + tiles):
                    last = STT(out=dst[:, k, :], in0=src[:, k, :], scalar=gain[:, k:k + 1], in1=root[:, 1, 0:cols],
                               op0=ALU.mult, op1=ALU.mult)
                return last

            dve.sem_inc(bank_free, 2)
            dve.sem_inc(o_taken, 2)
            dve.memset(ones[:], 1.0).then_inc(dve_set, 1)
            dve.memset(ue[:, :, 0:CW - 1], 0.0)
            dve.wait_ge(const_loaded, 16 * 5)
            dve.wait_ge(rooted, 1)
            dve.reciprocal(rms_x[:, 1, 0:NM], rms_x[:, 0, 0:NM])
            dve.drain()
            scale_by_norm(m_raw, m_raw, gm, rms_x, NM, 0, KT).then_inc(normed, 1)
            dve.wait_ge(xs_hi_done, 1)
            TT(xs_lo[:, :, 0:NM], m_raw[:], xs_hi[:, :, 0:NM].bitcast(F32), ALU.subtract).then_inc(xs_lo_done, 1)
            for n in range(4):
                split_lo(Place(n))
            dve.wait_ge(rooted, 2)
            dve.reciprocal(rms_x[:, 1, :], rms_x[:, 0, :])
            dve.drain()
            scale_by_norm(x_raw, x_raw, g1, rms_x, NT, 0, KT).then_inc(normed, 1)
            with dve.Fori(0, MEMK_BLOCKS // 4) as i:
                for j in range(2):
                    n = Place(MEMK0 + 2 * j, (4, i))
                    split_lo(n + 4)
                    split_lo(n + 5)
                    ended(n + 1)
                    move(tile_view(mk, i * 2 + j, 0, NM), ps[:, j, 0:NM]).then_inc(bank_free, 1)
            with dve.Fori(0, 2) as i:
                n = Place(MEMV0, (8, i))
                for r in range(8):
                    split_lo(n + (r + 4))
                ended(n + 7)
                move(mv[:, :, bass.ds(i * 512, 512)], ps[:, 0:2, :]).then_inc(bank_free, 2)
            for half, ready, done in ((slice(0, 8), (x_hi_half, 1), x_lo_half),
                                      (slice(8, 16), (xs_hi_done, 2), xs_lo_done)):
                dve.wait_ge(*ready)
                TT(xs_lo[:, half, :], x_raw[:, half, :], xs_hi[:, half, :].bitcast(F32), ALU.subtract
                   ).then_inc(done, 1)
            with dve.Fori(0, CT // 2) as i:
                for u in range(2):
                    n = Place(PROJ0 + 4 * u, (8, i))
                    for r in range(4):
                        split_lo(n + (r + 4))
                    dve.wait_ge(sig_done, i * 2 + (u + 1))
                    TT(tile_view(ue, i * 2 + u, CW - 1, NP), ps[:, 2 * u, 0:NP], sig[:, 0:NP], ALU.mult)
                    TT(ue[:, bass.ds(i * 2 + u, 1), PW:].rearrange("p o (b w) -> p (o b) w", b=NB)[:, :, CW - 1:SWD],
                       ps[:, 2 * u, NP:NT].rearrange("p (b t) -> p b t", b=NB),
                       sig[:, NP:NT].rearrange("p (b t) -> p b t", b=NB), ALU.mult).then_inc(bank_free, 2)
            dve.wait_ge(conv_prev_loaded, 16 * CT)
            STEPS = (PROJ_BLOCKS - 4 * CT) // (CT // 2)
            with dve.Fori(0, 2) as i:
                for pair in range(CT // 4):
                    def tap_view(cx, w):
                        ct = i * (CT // 2) + cx
                        sample = ue[:, bass.ds(ct, 1), PW:].rearrange("p o (b w) -> p (o b) w", b=NB)
                        return (tile_view(cc, ct, 0, NP), tile_view(ue, ct, w, NP),
                                cc[:, bass.ds(ct, 1), NP:NT].rearrange("p o (b t) -> p (o b) t", b=NB),
                                sample[:, :, w:w + NS], cw[:, bass.ds(i * (CT // 2 * CW) + (cx * CW + w), 1)])

                    for r in range(STEPS):
                        split_lo(Place(PROJ0 + 4 * CT + 4 + pair * STEPS + r, (STEPS * CT // 4, i)))
                        for w in range(r * CW // STEPS, (r + 1) * CW // STEPS):
                            dve.drain()
                            for cx in (2 * pair, 2 * pair + 1):
                                out_p, in_p, out_s, in_s, tap = tap_view(cx, w)
                                if w == 0:
                                    bias = cb[:, bass.ds(i * (CT // 2) + cx, 1)]
                                    TS(out_p, in_p, tap, bias, ALU.mult, ALU.add)
                                    last = TS(out_s, in_s, tap, bias, ALU.mult, ALU.add)
                                else:
                                    STT(out=out_p, in0=in_p, scalar=tap, in1=out_p, op0=ALU.mult, op1=ALU.add)
                                    last = STT(out=out_s, in0=in_s, scalar=tap, in1=out_s, op0=ALU.mult, op1=ALU.add)
                    last.then_inc(conv_done, 1)

            def gate(t, per=0, i=None):
                n = Place(GATE0 + 2 * t, *([(2 * per, i)] if per else []))
                split_lo(n + 4)
                split_lo(n + 5)

            dve.wait_ge(conv_stored, 16 * (1 + CT))
            dve.memset(to_row[:], 0.0)
            dve.drain()
            for t in range(HG):
                dve.memset(to_row[:, t, t:t + 1], 1.0)
                dve.tensor_copy(from_row[:, t, :], ident[0:HG, t:t + 1].to_broadcast([HG, P]))
            dve.wait_ge(ln_summed, 1)
            STT(out=cc[:], in0=strided(ps[:, 2, :], 0, [[0, CT], [1, NT]]), scalar=-1.0 / CC, in1=cc[:],
                op0=ALU.mult, op1=ALU.add).then_inc(ln_centered, 1)
            gate(0)
            dve.wait_ge(ln_rooted, 1)
            dve.reciprocal(rms_c[:, 1, :], rms_c[:, 0, :])
            dve.drain()
            TT(cc[:], cc[:], strided(rms_c[:, 1, :], 0, [[0, CT], [1, NT]]), ALU.mult).then_inc(ln_scaled, 1)
            gate(1)
            dve.wait_ge(ln_rooted, 2)
            dve.reciprocal(qk_r[:, :, 0:NM], qk_r[:, :, 0:NM])
            dve.drain()
            for h in range(MH):
                for half in range(2):
                    t = mk[:, 2 * h + half, :]
                    last = STT(out=t, in0=t, scalar=mkg[:, half:half + 1], in1=qk_r[:, h, 0:NM],
                               op0=ALU.mult, op1=ALU.mult)
            last.then_inc(mk_ready, 1)
            def row_reciprocal(k):
                rows = HG if k < 2 * G else 2
                dve.wait_ge(rooted, 3 + k)
                dve.reciprocal(r_row[0:rows, :], r_row[0:rows, :]).then_inc(row_ready, 1)

            row_reciprocal(0)
            for k in range(2 * G + 2):
                gate(2 + k)
                dve.wait_ge(row_spread, k + 1)
                if k < 2 * G:
                    g, first, gain = k // 2, (k // 2) * 12 + (k % 2) * HG, (kg if k % 2 else qg)
                    last = STT(out=hb[:, first:first + HG, :], in0=hb[:, first:first + HG, :], scalar=gain[:, g:g + 1],
                               in1=ps[:, 3:7, 0:NT], op0=ALU.mult, op1=ALU.mult)
                else:
                    for half in range(2):
                        first = 36 + (k - 2 * G) * HG + half
                        t = hb[:, first:first + 3:2, :]
                        last = STT(out=t, in0=t, scalar=mqg[:, half:half + 1], in1=ps[:, 3:5, 0:NT],
                                   op0=ALU.mult, op1=ALU.mult)
                last.then_inc(normed, 1)
                if k < 2 * G + 1:
                    row_reciprocal(k + 1)
            gate(10)
            dve.wait_ge(mem_stored, 16 * 2)
            dve.wait_ge(conv_stored, 16 * (1 + CT))
            for g in range(G):
                for f in range(4):
                    m = 4 * g + f
                    dve.wait_ge(vt_turned, m + 1)
                    if f < 2:
                        dst = vnp[:, f, g * HG:(g + 1) * HG, :].rearrange("p h d -> p (h d)")
                        src = ps[:, 2 + f, :]
                    else:
                        dst = nnew[:, f - 2, g * HG * P:(g + 1) * HG * P]
                        src = ps[0:NB * NS, 2 + f, :]
                    dve.tensor_copy(dst, src).then_inc(vt_copied, 1)
            gate(11)

            def negmax(out, src):
                return dve.tensor_reduce(out, src, AX.X, ALU.max, negate=True)

            dve.wait_ge(dist_p_loaded, 16)
            dve.drain()
            with dve.Fori(0, HG) as h:
                dve.tensor_copy(q_st[:], hb[:, 0:36, :].rearrange("p (g k) n -> p g k n", g=G)[
                    :, :, bass.ds(h, 1), 0:NP].rearrange("p g o n -> p (g o) n"))
                for st in range(2):
                    last = dve.tensor_copy(v_st[:, st], vnp[:, st].rearrange("p (g h) d -> p g h d", g=G)[
                        :, :, bass.ds(h, 1), :].rearrange("p g o d -> p (g o) d"))
                last.then_inc(a_staged, 1)
                dve.wait_ge(a_scored, h + 1)
                for g in range(G):
                    m = slope[:, bass.ds(h + g * HG, 1)]
                    STT(out=sS[:, g * P:(g + 1) * P], in0=dpr[:, 0, g, 0:P], scalar=m,
                        in1=ps[:, 2, g * P:(g + 1) * P], op0=ALU.mult, op1=ALU.add)
                    src = ps[:, 3 + g // 2, (g % 2) * NP:(g % 2 + 1) * NP]
                    STT(out=sS[:, G * P + g * NP:G * P + (g + 1) * NP], in0=dpr[:, 1, g, :], scalar=m, in1=src,
                        op0=ALU.mult, op1=ALU.add)
                dve.drain()
                negmax(stat[:, 0:1], sS[:, 0:G * P])
                negmax(stat[:, 1:2], sS[:, G * P:G * (P + NP)]).then_inc(a_biased, 1)
                dve.wait_ge(a_exped, h + 1)
                dve.reciprocal(stat[:, 4:6], stat[:, 2:4])
                dve.drain()
                TS(sS[:, 0:G * P], sS[:, 0:G * P], stat[:, 4:5], None, ALU.mult)
                TS(sS[:, G * P:G * (P + NP)], sS[:, G * P:G * (P + NP)], stat[:, 5:6], None, ALU.mult
                   ).then_inc(a_probs, 1)
                gate(WIN_G0, WIN_G, h)
                gate(WIN_G0 + 1, WIN_G, h)
                dve.wait_ge(a_mixed, h + 1)
                move(tile_view(hb, h + 8, 0, NP), ps[:, 2, 0:NP]).then_inc(a_kept, 1)

            dve.wait_ge(km_prompt_loaded, 16 * 2)
            with dve.Fori(0, MH) as h:
                dve.tensor_copy(mq_st[:], hb[:, bass.ds(h * 2 + 36, 2), 0:NP])
                dve.tensor_copy(mv_st[:], km[:, 1, :].rearrange("p (s n) -> p s n", s=2)[:, :, bass.ds(h * MD, MD)]
                                ).then_inc(m_staged, 1)
                dve.wait_ge(m_scored, h + 1)
                negmax(stat[:, 0:2], ps[:, 2, :].rearrange("p (q n) -> p q n", q=2)).then_inc(m_maxed, 1)
                dve.wait_ge(m_exped, h + 1)
                dve.reciprocal(stat[:, 4:6], stat[:, 2:4])
                dve.drain()
                TS(sS[:, 0:NM], sS[:, 0:NM], stat[:, 4:5], None, ALU.mult)
                TS(sS[:, NM:2 * NM], sS[:, NM:2 * NM], stat[:, 5:6], None, ALU.mult).then_inc(m_probs, 1)
                gate(MEM_G0, MEM_G, h)
                gate(MEM_G0 + 1, MEM_G, h)
                dve.wait_ge(m_mixed, h + 1)
                move(hb[:, bass.ds(h * 2 + 36, 2), 0:NP],
                                ps[:, 4, :].rearrange("p (d n) -> p d n", d=2)).then_inc(m_kept, 1)

            dve.memset(zm[:], 0.0)
            dve.drain()
            with dve.Fori(0, 2) as i:
                def mask_memory(part, bq, src_of):
                    dve.wait_ge(zm_used, i * 8 + (part * 4 + bq + 2))
                    for half in range(2):
                        last = move(strided(zm[:, half, :, :], 0, [[DIAG, MH], [1, NS]]), src_of(half))
                    last.then_inc(zm_set, 1)

                for bq in range(4):
                    mask_memory(0, bq, lambda half: hb[:, 36 + half:43 + half:2, bass.ds(i * 32 + (NP + NS * bq), NS)])
                    if bq == 2:
                        gate(MEMS_G0, MEMS_G, i)
                dve.wait_ge(zm_used, i * 8 + 6)
                negmax(stat[:, 0:1], ps[:, 2, 0:NM]).then_inc(n_maxed, 1)
                dve.wait_ge(n_exped, i + 1)
                dve.reciprocal(stat[:, 4:5], stat[:, 2:3])
                dve.drain()
                TS(sS[:, 0:NM], sS[:, 0:NM], stat[:, 4:5], None, ALU.mult).then_inc(n_probs, 1)
                gate(MEMS_G0 + 1, MEMS_G, i)
                dve.wait_ge(n_copied, i + 1)
                for bq in range(4):
                    mask_memory(1, bq, lambda half: pT[:, half * P + 32 * bq:half * P + 32 * bq + 32].rearrange(
                        "p (h t) -> p h t", h=MH))
                    if bq == 1:
                        gate(MEMS_G0 + 2, MEMS_G, i)
                    if bq == 3:
                        gate(MEMS_G0 + 3, MEMS_G, i)
                gate(MEMS_G0 + 4, MEMS_G, i)
                dve.wait_ge(n_back, i + 1)
                for dt in range(2):
                    last = move(
                        hb[:, 36 + dt:43 + dt:2, bass.ds(i * 32 + NP, 32)].rearrange("p h (b t) -> p b h t", b=4),
                        ps[:, 5, dt * P:(dt + 1) * P].rearrange("p (b h t) -> p b h t", b=4, h=MH))
                last.then_inc(n_kept, 1)
                gate(MEMS_G0 + 5, MEMS_G, i)

            dve.memset(z[:], 0.0)
            dve.memset(z4[:], 0.0)
            dve.wait_ge(dist_s_loaded, 16)
            dve.drain()
            NEW_DIAG = [[P + NS, HG], [32, 4], [1, NS]]
            with dve.Fori(0, 2) as i:
                dve.wait_ge(z_used, i * 10 + 1)
                for g in range(G):
                    last = move(strided(z4[:, :, :, :], g * HG * P, NEW_DIAG),
                                hb[:, g * 12:g * 12 + HG, bass.ds(i * 32 + NP, 32)].rearrange(
                                    "p h (b t) -> p h b t", b=4))
                last.then_inc(z_set, 1)
                for bq in range(4):
                    cols = bass.ds(i * 32 + (NP + NS * bq), NS)
                    dve.wait_ge(z_used, i * 10 + (bq + 2))
                    for dst, src in z_views(z, lambda g: hb[:, g * 12:g * 12 + HG, cols]):
                        last = move(dst, src)
                    last.then_inc(z_set, 1)
                    if bq == 1:
                        gate(WINS_G0, WINS_G, i)
                dve.wait_ge(z_used, i * 10 + 6)
                TT(sT[:], ps[:, 2, 0:SAMPLE_COLS], dsm[:], ALU.add)
                dve.drain()
                negmax(stat2[:, 0:1], sT[:]).then_inc(s_maxed, 1)
                dve.wait_ge(s_exped, i + 1)
                dve.reciprocal(stat2[:, 2:3], stat2[:, 1:2])
                dve.drain()
                TS(sT[:], sT[:], stat2[:, 2:3], None, ALU.mult).then_inc(s_probs, 1)
                gate(WINS_G0 + 1, WINS_G, i)
                dve.wait_ge(s_copied, i + 1)
                for g in range(G):
                    last = dve.tensor_copy(strided(z4[0:4 * NS, :, :, :], g * HG * P, NEW_DIAG),
                                           pTn[:, g * P:(g + 1) * P].rearrange("p (b h t) -> p h b t", b=4, h=HG))
                last.then_inc(z_set, 1)
                for bq in range(4):
                    def probs_of(g):
                        return pTs[:, g * P + 32 * bq:g * P + 32 * bq + 32].rearrange("p (h t) -> p h t", h=HG)

                    dve.wait_ge(z_used, i * 10 + (bq + 7 if bq else 6))
                    for dst, src in z_views(z, probs_of):
                        last = dve.tensor_copy(dst, src)
                    last.then_inc(z_set, 1)
                    if bq == 1:
                        gate(WINS_G0 + 2, WINS_G, i)
                dve.wait_ge(z_used, i * 10 + 11)
                dve.tensor_copy(osb[:], ps[:, 5, 0:P])
                dve.drain()
                TT(osb[:], osb[:], ps[:, 5, P:2 * P], ALU.add).then_inc(s_out, 1)
                gate(WINS_G0 + 3, WINS_G, i)
                dve.wait_ge(s_back, i + 1)
                move(hb[:, 8:8 + HG, bass.ds(i * 32 + NP, 32)].rearrange("p h (b t) -> p b h t", b=4),
                     ps[:, 6, 0:P].rearrange("p (b h t) -> p b h t", b=4, h=HG)).then_inc(s_kept, 1)

            dve.wait_ge(xs_hi_done, 3)
            TT(xs_lo[:, 0:CT, :], cc[:], xs_hi[:, 0:CT, :].bitcast(F32), ALU.subtract).then_inc(xs_lo_done, 1)
            dve.wait_ge(xs_hi_done, 4)
            TT(xs_lo[:, CT:2 * CT, :], hb[:, 36:44, :], xs_hi[:, CT:2 * CT, :].bitcast(F32), ALU.subtract
               ).then_inc(xs_lo_done, 1)
            dve.wait_ge(osw_hi_done, 1)
            TT(osw_lo[:], hb[:, 8:8 + HG, :], osw_hi[:].bitcast(F32), ALU.subtract).then_inc(osw_lo_done, 1)
            with dve.Fori(0, 2) as i:
                n = Place(OPROJ0, (20, i))
                for m in range(KT // 2):
                    blocks = range(3) if m % 2 == 0 else range(3, 5)
                    for r in blocks:
                        split_lo(n + ((m // 2) * 5 + r + 4))
                    ended(n + ((m // 2) * 5 + blocks[-1]))
                    dve.wait_ge(gl_loaded[m % 2], i * 64 + 16 * (m // 2 + 1))
                    u = m % 2
                    TT(mt[:, 0, :], gl[:, u, 0, :], ps[:, 2 + 3 * u, 0:NT], ALU.mult)
                    TT(mt[:, 1, :], gl[:, u, 1, :], ps[:, 4 + 3 * u, 0:NT], ALU.mult)
                    TT(mt[:, 2, :], gl[:, u, 2, :], ps[:, 3 + 3 * u, 0:NT], ALU.mult).then_inc(o_taken, 1)
                    dve.drain()
                    TT(mt[:, 0, :], mt[:, 0, :], mt[:, 1, :], ALU.add)
                    dve.drain()
                    TT(mt[:, 3, :], mt[:, 0, :], mt[:, 2, :], ALU.add).then_inc(merged, 1)
                    dve.wait_ge(merged_hi, i * 8 + (m + 1))
                    TT(tile_view(xs2_lo, i * 8 + m), mt[:, 3, :], tile_view(xs2_hi, i * 8 + m).bitcast(F32),
                       ALU.subtract).then_inc(merged_lo, 1)

            def add_tiles(n, m):
                split_lo(n + 4)
                split_lo(n + 5)
                ended(n + 1)
                t = tile_view(acc, m)
                TT(t, t, ps[:, (n.const // 2) % 2, 0:NT], ALU.add).then_inc(bank_free, 1)

            dve.wait_ge(acc_loaded, 16)
            with dve.Fori(0, OUT_BLOCKS // 4) as i:
                for j in range(2):
                    add_tiles(Place(OUT0 + 2 * j, (4, i)), i * 2 + j)
            dve.wait_ge(rooted, 11)
            dve.reciprocal(rms_h[:, 1, :], rms_h[:, 0, :])
            dve.drain()
            for c in range(4):
                scale_by_norm(qT, acc, g2, rms_h, NT, 4 * c, 4).then_inc(normed, 1)
            for c in range(4):
                part = slice(4 * c, 4 * c + 4)
                dve.wait_ge(xs_hi_done, 5 + c)
                TT(xs_lo[:, part, :], qT[:, part, :], xs_hi[:, part, :].bitcast(F32), ALU.subtract
                   ).then_inc(xs_lo_done, 1)
            with dve.Fori(0, WQ_BLOCKS // 4) as i:
                for r in range(4):
                    split_lo(Place(WQ0 + 4 + r, (4, i)))

            def select(n, h):
                dve.tensor_copy(pq_st[:], qT[:, bass.ds(h * 2, 2), :]).then_inc(t_staged, 1)
                split_lo(n + 4)
                split_lo(n + 5)
                split_lo(n + 6)
                dve.wait_ge(t_scored, h + 1)
                split_lo(n + 7)
                six = [slice(q * PK, (q + 1) * PK) for q in range(6)]
                scores = [ps[:, 2 + q // 3, (q % 3) * PK:(q % 3 + 1) * PK] for q in range(6)]
                for q in range(6):
                    dve.max(tv[:, q, 0:8], scores[q])
                dve.drain()
                for q in range(6):
                    dve.max_index(tiu[:, q, 0:8], tv[:, q, 0:8], scores[q])
                    dve.match_replace(tW[:, six[q]], tv[:, q, 0:8], scores[q], -3.0e38)
                dve.drain()
                for q in range(6):
                    dve.max(tv[:, q, 8:16], tW[:, six[q]])
                dve.drain()
                split_lo(n + 8)
                split_lo(n + 9)
                for q in range(6):
                    dve.max_index(tiu[:, q, 8:16], tv[:, q, 8:16], tW[:, six[q]])
                TT(tS[:].rearrange("p (t a b) -> p t a b", t=3, a=TOPK),
                   strided(tv[:, :, :], 0, [[2 * TOPK, 3], [1, TOPK], [0, TOPK]]),
                   strided(tv[:, :, :], TOPK, [[2 * TOPK, 3], [0, TOPK], [1, TOPK]]), ALU.add)
                dve.drain()
                dve.tensor_copy(tif[:], tiu[:])
                three = [slice(t * 2 * PK, (t + 1) * 2 * PK) for t in range(3)]
                for t in range(3):
                    dve.max(cv[:, t, 0:8], tS[:, three[t]])
                dve.drain()
                TS(tz[:, 0:3], cv[:, :, 0], -1.0, None, ALU.mult)
                for t in range(3):
                    dve.max_index(ci[:, t, 0:8], cv[:, t, 0:8], tS[:, three[t]])
                    dve.match_replace(tW[:, three[t]], cv[:, t, 0:8], tS[:, three[t]], -3.0e38)
                dve.drain()
                for t in range(3):
                    last = dve.max(cv[:, t, 8:16], tW[:, three[t]])
                last.then_inc(t_picked, 1)
                dve.drain()
                for t in range(3):
                    dve.max_index(ci[:, t, 8:16], cv[:, t, 8:16], tW[:, three[t]])
                dve.drain()
                split_lo(n + 10)
                split_lo(n + 11)
                TS(cab[:, 0], ci[:], 4, None, ALU.logical_shift_right)
                TS(cab[:, 1], ci[:], TOPK - 1, None, ALU.bitwise_and)
                dve.drain()
                dve.tensor_copy(cabf[:], cab[:])
                dve.drain()
                for half in range(2):
                    TT(eq[:], strided(iota16[:, :], 0, [[0, 3], [0, TOPK], [1, TOPK]]),
                       strided(cabf[:, :, :, :], half * 3 * TOPK, [[TOPK, 3], [1, TOPK], [0, TOPK]]), ALU.is_equal)
                    dve.drain()
                    TT(eq[:], eq[:], strided(tif[:, :, :], half * TOPK, [[2 * TOPK, 3], [0, TOPK], [1, TOPK]]),
                       ALU.mult)
                    dve.drain()
                    dve.tensor_reduce(R[:, :, half, bass.ds(h, 1), :].rearrange("p t o k -> p t (o k)"), eq[:],
                                      AX.X, ALU.add)
                    dve.drain()
                split_lo(n + 12)
                split_lo(n + 13)
                dve.wait_ge(t_exped, h + 1)
                dve.reciprocal(tz[:, 6:9], tz[:, 3:6])
                dve.drain()
                TT(R[:, :, 2, bass.ds(h, 1), :].rearrange("p t o k -> p t (o k)"), ce[:],
                   strided(tz[:, :], 6, [[1, 3], [0, TOPK]]), ALU.mult).then_inc(r_done, 1)

            dve.wait_ge(bank_free, taken(WQ_T + KT - 1))
            with dve.Fori(0, PH // 2) as h2:
                for u in range(2):
                    select(Place(U0 + 2 * SELECT_TILES * u, (4 * SELECT_TILES, h2)), h2 * 2 + u)

            dve.wait_ge(r_turned, 1)
            dve.tensor_copy(T[:, :, 0:P], ps[:, 2, 0:3 * P].rearrange("p (k n) -> p k n", k=3))
            dve.tensor_copy(T[:, :, P:2 * P], ps[:, 3, 0:3 * P].rearrange("p (k n) -> p k n", k=3))
            dve.tensor_copy(T[:, :, 2 * P:NT], ps[:, 4, 0:3 * P].rearrange("p (k n) -> p k n", k=3)[:, :, 2 * P - 192:P]
                            ).then_inc(t_set, 1)
            dve.drain()
            with dve.Fori(0, NT // 64) as tb:
                for m in range(16):
                    n = Place(U0 + 2 * SPREAD_U + 2 * m, (32, tb))
                    dve.wait_ge(hot_used, tb * 16 + (m + 1))
                    for tk in range(4):
                        tok = bass.ds(tb * 64 + (4 * m + tk), 1)
                        TS(hot[:, m % 2, tk, 0, :], iota[:], T[:, 0, tok], None, ALU.is_equal)
                        last = TS(hot[:, m % 2, tk, 1, :], iota[:], T[:, 1, tok], T[:, 2, tok],
                                  ALU.is_equal, ALU.mult)
                    last.then_inc(hot_set, 1)
                    split_lo(n + 4)
                    split_lo(n + 5)

            def c_make(step, loaded):
                p = step.const % 8
                c, ii = (p // 2) % 2, 2 * (p % 2)
                dve.wait_ge(chunk_loaded[c], loaded.value(32, 32))
                if step.const >= 2:
                    dve.wait_ge(c_hi, step.value(plus=-1))
                TT(cf[:, p % 2].rearrange("p i (b t) -> p i b t", t=32),
                   actc[:, c, ii:ii + 2, :].rearrange("p i (b t) -> p i b t", t=32),
                   gc[:, c, :, ii:ii + 2, :].rearrange("p b i t -> p i b t"), ALU.mult).then_inc(c_made, 1)

            def c_rest(step, hi, lo):
                dve.wait_ge(c_hi, step.value(plus=1))
                TT(lo, cf[:, step.const % 2], hi.bitcast(F32), ALU.subtract).then_inc(c_lo, 1)

            for p in range(8):
                n = Place(U0 + 2 * (LAST_U + p))
                c_make(Place(p), Place(p // 4))
                split_lo(n + 4)
                c_rest(Place(p), xs2_hi[:, 2 * p:2 * p + 2, :], xs2_lo[:, 2 * p:2 * p + 2, :])
                split_lo(n + 5)

            def v_group(gg, group, hi, lo):
                def at(const, per_i, per_gg, i):
                    return Place(const, (per_i, i), *([(per_gg, gg)] if gg is not None else []))

                with dve.Fori(0, 2) as i:
                    for p in range(4):
                        n = at(V0 + group * 32 + 4 * p, 16, 64, i)
                        step = at(8 + group * 8 + p, 4, 16, i)
                        two = bass.ds(i * 8 + 2 * p, 2)
                        c_make(step, at(2 + 2 * group, 1, 4, i))
                        split_lo(n + 4)
                        c_rest(step, hi[:, two, :], lo[:, two, :])
                        split_lo(n + 5)
                        ended(n + 1)
                        t = tile_view(acc, i * 8 + 2 * p)
                        TT(t, t, ps[:, 0, 0:NT], ALU.add).then_inc(bank_free, 1)
                        split_lo(n + 6)
                        split_lo(n + 7)
                        ended(n + 3)
                        t = tile_view(acc, i * 8 + 2 * p + 1)
                        TT(t, t, ps[:, 1, 0:NT], ALU.add).then_inc(bank_free, 1)
                dve.drain()

            with dve.Fori(0, 3) as gg:
                v_group(gg, 0, xs_hi, xs_lo)
                v_group(gg, 1, xs2_hi, xs2_lo)
            v_group(None, 6, xs_hi, xs_lo)
            with dve.Fori(0, 7) as i:
                for j in range(2):
                    add_tiles(Place(V0 + 7 * 32 + 2 * j, (4, i)), i * 2 + j)
            for j in range(2):
                ended(Place(END - 4 + 2 * j + 1))
                TT(acc[:, KT - 2 + j, :], acc[:, KT - 2 + j, :], ps[:, j, 0:NT], ALU.add).then_inc(bank_free, 1)

        @block.tensor
        def _(pe):
            def three(out, a_hi, a_lo, b_hi, b_lo, start, stop):
                pe.matmul(out, a_hi, b_hi, start=start, stop=False)
                pe.matmul(out, a_hi, b_lo, start=False, stop=False)
                return pe.matmul(out, a_lo, b_hi, start=False, stop=stop)

            def stream(n, out, hi, lo, first, start, stop, cols=NT, tiles=8, at=0):
                s = n.const % 4
                for k in range(tiles):
                    w = slice((at + k) * P, (at + k + 1) * P)
                    last = three(out, w_hi[:, s, w], w_lo[:, s, w], hi[:, first + k, 0:cols], lo[:, first + k, 0:cols],
                                 start and k == 0, stop and k == tiles - 1)
                return last

            def split_done(n):
                pe.wait_ge(lo_done, n.value(plus=1))

            def project(n, tile, bank, hi, lo, cols=NT, second_half=None):
                pe.wait_ge(bank_free, tile.value(plus=1))
                for half in range(2):
                    split_done(n + half)
                    if half and second_half:
                        pe.wait_ge(*second_half)
                    stream(n + half, ps[:, bank, 0:cols], hi, lo, 8 * half, half == 0, half == 1, cols
                           ).then_inc(w_released, 1)

            pe.sem_inc(kv_used, KV_SLOTS)
            pe.sem_inc(hot_used, 2)
            pe.sem_inc(zm_used, 2)
            pe.sem_inc(z_used, 1)
            pe.wait_ge(dve_set, 1)

            def sum_squares(count, src, bank, cols):
                for c in range(4):
                    pe.wait_ge(sq_done, count + c + 1)
                    for k in range(4):
                        last = pe.matmul(ps[:, bank, 0:cols], ones[:], src[:, k, 0:cols],
                                         start=c == 0 and k == 0, stop=c == 3 and k == 3)
                    last.then_inc(sq_summed, 1)

            sum_squares(0, sq4, 2, NM)
            sum_squares(4, sq4, 3, NT)
            pe.wait_ge(xs_lo_done, 1)
            with pe.Fori(0, MEMK_BLOCKS // 4) as i:
                for j in range(2):
                    project(Place(MEMK0 + 2 * j, (4, i)), Place(MEMK_T + j, (2, i)), j, xs_hi, xs_lo, NM)
            with pe.Fori(0, 2) as i:
                pe.wait_ge(bank_free, i * 2 + (MEMV_T + 2))
                for r in range(8):
                    n = Place(MEMV0 + r, (8, i))
                    split_done(n)
                    for kk in range(2):
                        k, w = 2 * r + kk, slice(kk * 512, (kk + 1) * 512)
                        for tt in range(2):
                            t = slice(tt * P, (tt + 1) * P)
                            last = three(ps[:, tt, :], xs_hi[:, k, t], xs_lo[:, k, t], w_hi[:, r % 4, w],
                                         w_lo[:, r % 4, w], k == 0, k == KT - 1)
                    last.then_inc(w_released, 1)
            pe.wait_ge(x_lo_half, 1)
            pe.wait_ge(bank_free, taken(PROJ_T - 1))
            with pe.Fori(0, CT // 2) as i:
                for j in range(4):
                    project(Place(PROJ0 + 2 * j, (8, i)), Place(PROJ_T - 2 + j, (4, i)), j, xs_hi, xs_lo,
                            second_half=(xs_lo_done, 2))
            with pe.Fori(0, PROJ_BLOCKS // 4 - CT) as i:
                for j in range(2):
                    project(Place(PROJ0 + 4 * CT + 2 * j, (4, i)), Place(PROJ_T + 2 * CT + j, (2, i)), j, xs_hi, xs_lo)

            def gate(t, per=0, i=None):
                project(Place(GATE0 + 2 * t, *([(2 * per, i)] if per else [])),
                        Place(GATE_T + t, *([(per, i)] if per else [])), t % 2, xs_hi, xs_lo)

            pe.wait_ge(conv_done, CT // 2)
            for ct in range(CT):
                last = pe.matmul(ps[:, 2, 0:NT], ones[:], cc[:, ct, :], start=ct == 0, stop=ct == CT - 1)
            last.then_inc(ln_summed, 1)
            gate(0)
            for c in range(2):
                pe.wait_ge(ln_squared, c + 1)
                for k in range(4):
                    last = pe.matmul(ps[:, 3, 0:NT], ones[:], qk_sq[:, k, :],
                                     start=c == 0 and k == 0, stop=c == 1 and k == 3)
                last.then_inc(ln_summed, 1)
            gate(1)
            for c in range(2):
                pe.wait_ge(ln_squared, 2 + c + 1)
                for h in range(2):
                    for half in range(2):
                        last = pe.matmul(ps[:, 4 + c, h * NM:(h + 1) * NM], ones[:], qk_sq[:, 2 * h + half, 0:NM],
                                         start=half == 0, stop=half == 1)
                last.then_inc(ln_summed, 1)
            def row_sums(k):
                pe.wait_ge(sq_done, 8 + k + 1)
                for t in range(HG):
                    row = t if k < 2 * G else t // 2
                    last = pe.matmul(ps[0:HG, 2, 0:NT], to_row[:, row, :], qk_sq[:, t, :], start=t == 0,
                                     stop=t == HG - 1)
                last.then_inc(sq_summed, 1)

            row_sums(0)
            for k in range(2 * G + 2):
                gate(2 + k)
                pe.wait_ge(row_ready, k + 1)
                for t in range(HG if k < 2 * G else 2):
                    last = pe.matmul(ps[:, 3 + t, 0:NT], from_row[:, t, :], r_row[:], start=True, stop=True)
                last.then_inc(row_spread, 1)
                if k < 2 * G + 1:
                    row_sums(k + 1)
            gate(10)

            pe.wait_ge(normed, 2 + 2 * G + 2)
            for g in range(G):
                for f in range(4):
                    m = 4 * g + f
                    if m >= 4:
                        pe.wait_ge(vt_copied, m - 3)
                    for h in range(HG):
                        tile = g * 12 + (4 if f == 2 else 8) + h
                        cols = slice(f * P, (f + 1) * P) if f < 2 else slice(NP, NT)
                        rows = cols.stop - cols.start
                        last = pe.transpose(ps[0:rows, 2 + f, h * P:(h + 1) * P], hb[:, tile, cols], ident[:])
                    last.then_inc(vt_turned, 1)
            gate(11)

            with pe.Fori(0, HG) as h:
                pe.wait_ge(a_staged, h + 1)
                for g in range(G):
                    def keys(n):
                        return hb[:, bass.ds(h + (g * 12 + HG), 1), 0:n].rearrange("p o n -> p (o n)")

                    pe.matmul(ps[:, 2, g * P:(g + 1) * P], q_st[:, g, 0:P], keys(P), start=True, stop=True)
                    last = pe.matmul(ps[:, 3 + g // 2, (g % 2) * NP:(g % 2 + 1) * NP], q_st[:, g, P:NP], keys(NP),
                                     start=True, stop=True)
                last.then_inc(a_scored, 1)
                gate(WIN_G0, WIN_G, h)
                pe.wait_ge(a_probs, h + 1)
                for g in range(G):
                    pe.transpose(ps[:, 5, g * P:(g + 1) * P], sS[:, g * P:(g + 1) * P], ident[:])
                for c in range(2 * G):
                    src = sS[:, (G + c) * P:(G + c + 1) * P]
                    last = pe.transpose(ps[:, 6 + c // 3, (c % 3) * P:(c % 3 + 1) * P], src, ident[:])
                last.then_inc(a_turned, 1)
                gate(WIN_G0 + 1, WIN_G, h)
                pe.wait_ge(a_copied, h + 1)
                for g in range(G):
                    pe.matmul(ps[:, 2, 0:P], v_st[:, 0, g, :], pT[:, g * P:(g + 1) * P], start=g == 0, stop=g == G - 1)
                for c in range(2 * G):
                    last = pe.matmul(ps[:, 2, P:NP], v_st[:, c % 2, c // 2, :], pT[:, (G + c) * P:(G + c + 1) * P],
                                     start=c == 0, stop=c == 2 * G - 1)
                last.then_inc(a_mixed, 1)

            pe.wait_ge(km_prompt_loaded, 16 * 2)
            with pe.Fori(0, MH) as h:
                pe.wait_ge(m_staged, h + 1)
                for qb in range(2):
                    for half in range(2):
                        last = pe.matmul(ps[:, 2, qb * NM:(qb + 1) * NM], mq_st[:, half, qb * P:(qb + 1) * P],
                                         km[:, 0, bass.ds(h * (2 * NM) + half * NM, NM)],
                                         start=half == 0, stop=half == 1)
                last.then_inc(m_scored, 1)
                gate(MEM_G0, MEM_G, h)
                pe.wait_ge(m_probs, h + 1)
                for qb in range(2):
                    for st in range(2):
                        last = pe.transpose(ps[:, 3, st * NP + qb * P:st * NP + (qb + 1) * P],
                                            sS[:, qb * NM + st * P:qb * NM + (st + 1) * P], ident[:])
                last.then_inc(m_turned, 1)
                gate(MEM_G0 + 1, MEM_G, h)
                pe.wait_ge(m_copied, h + 1)
                for dt in range(2):
                    for st in range(2):
                        last = pe.matmul(ps[:, 4, dt * NP:(dt + 1) * NP], mv_st[:, st, dt * P:(dt + 1) * P],
                                         pT[:, st * NP:(st + 1) * NP], start=st == 0, stop=st == 1)
                last.then_inc(m_mixed, 1)

            with pe.Fori(0, 2) as i:
                for part in range(2):
                    for bq in range(4):
                        c = part * 4 + bq
                        pe.wait_ge(km_loaded[bq % 2], i * 64 + 16 * (c // 2 + 1))
                        pe.wait_ge(zm_set, i * 8 + (c + 1))
                        for h in range(MH):
                            for half in range(2):
                                at = (2 * h + half) * NM if part == 0 else half * MH * MD + h * MD
                                last = pe.matmul(ps[32 * bq:32 * bq + 32, 2 + 2 * part, 0:NM], zm[:, half, h, :],
                                                 km[:, bq % 2, at:at + NM], start=h == 0 and half == 0,
                                                 stop=h == MH - 1 and half == 1, tile_position=(0, 32 * bq))
                        last.then_inc(zm_used, 1)
                        if c in (1, 5, 7):
                            gate(MEMS_G0 + {1: 0, 5: 2, 7: 3}[c], MEMS_G, i)
                    if part == 0:
                        gate(MEMS_G0 + 1, MEMS_G, i)
                        pe.wait_ge(n_probs, i + 1)
                        for st in range(2):
                            last = pe.transpose(ps[:, 3, st * P:(st + 1) * P], sS[:, st * P:(st + 1) * P], ident[:])
                        last.then_inc(n_turned, 1)
                pe.wait_ge(n_out, i + 1)
                for dt in range(2):
                    last = pe.transpose(ps[:, 5, dt * P:(dt + 1) * P], sS[:, NM + dt * P:NM + (dt + 1) * P], ident[:])
                last.then_inc(n_back, 1)
                gate(MEMS_G0 + 4, MEMS_G, i)
                gate(MEMS_G0 + 5, MEMS_G, i)

            GROUP_OF = [g for g in range(G) for _ in range(min(DILATIONS[g], NS))]
            with pe.Fori(0, 2) as i:
                for part in range(2):
                    pe.wait_ge(z_set, i * 10 + (5 * part + 1))
                    if part:
                        pe.wait_ge(vnew_loaded, i * 16 + 16)
                    for g in range(G):
                        for h in range(HG):
                            if part == 0:
                                at = G * P + 32 * g
                                last = pe.matmul(ps[:, 2, at:at + 32], z4[:, g, h, :],
                                                 hb[:, g * 12 + HG + h, bass.ds(i * 32 + NP, 32)],
                                                 start=h == 0, stop=h == HG - 1)
                            else:
                                last = pe.matmul(ps[:, 5, P:2 * P], z4[0:4 * NS, g, h, :],
                                                 vnew[:, (g * HG + h) * P:(g * HG + h + 1) * P],
                                                 start=g == 0 and h == 0, stop=g == G - 1 and h == HG - 1)
                    last.then_inc(z_used, 1)
                    for bq in range(4):
                        rows = slice(32 * bq, 32 * bq + 32)
                        where = (0, 32 * bq)
                        c = part * 4 + bq
                        pe.wait_ge(z_set, i * 10 + (5 * part + bq + 2))
                        for u in range(UNITS):
                            m = c * UNITS + u
                            g = GROUP_OF[u]
                            pe.wait_ge(kv_loaded[m % KV_SLOTS], i * (16 * UNITS) + 16 * (m // KV_SLOTS + 1))
                            for h in range(HG):
                                kv_h = kv[:, m % KV_SLOTS, h * P:(h + 1) * P]
                                if part == 0:
                                    first = h == 0 and (u == 0 or GROUP_OF[u - 1] != g)
                                    final = h == HG - 1 and (u == UNITS - 1 or GROUP_OF[u + 1] != g)
                                    last = pe.matmul(ps[rows, 2, g * P:(g + 1) * P], z[:, u, h, :], kv_h,
                                                     start=first, stop=final, tile_position=where)
                                else:
                                    last = pe.matmul(ps[rows, 5, 0:P], z[:, u, h, :], kv_h,
                                                     start=u == 0 and h == 0, stop=u == UNITS - 1 and h == HG - 1,
                                                     tile_position=where)
                            last.then_inc(kv_used, 1)
                        pe.drain().then_inc(z_used, 1)
                        if bq == 0:
                            gate(WINS_G0 + 2 * part, WINS_G, i)
                    if part == 0:
                        gate(WINS_G0 + 1, WINS_G, i)
                        pe.wait_ge(s_probs, i + 1)
                        for g in range(G):
                            pe.transpose(ps[:, 3, g * P:(g + 1) * P], sT[:, g * P:(g + 1) * P], ident[:])
                        for g in range(G):
                            last = pe.transpose(ps[0:32, 4, g * P:(g + 1) * P],
                                                sT[:, G * P + g * 32:G * P + (g + 1) * 32], ident[:])
                        last.then_inc(s_turned, 1)
                gate(WINS_G0 + 3, WINS_G, i)
                pe.wait_ge(s_out, i + 1)
                pe.transpose(ps[:, 6, 0:P], osb[:], ident[:]).then_inc(s_back, 1)

            pe.wait_ge(bank_free, taken(GATE_T + 3 * KT - 1))
            pe.wait_ge(xs_lo_done, 3)
            with pe.Fori(0, 2) as i:
                for pair in range(KT // 4):
                    n = Place(OPROJ0 + 5 * pair, (20, i))
                    for u in range(2):
                        pe.wait_ge(o_taken, i * 8 + (2 * pair + u + 1))
                        if u:
                            pe.wait_ge(osw_lo_done, 1)
                            split_done(n + 2)
                            for v in range(2):
                                last = stream(n + 2, ps[:, 4 + 3 * v, 0:NT], osw_hi, osw_lo, 0, True, True,
                                              tiles=4, at=4 * v)
                            last.then_inc(w_released, 1)
                        for branch in range(2):
                            r = 3 * u + branch
                            split_done(n + r)
                            if branch:
                                pe.wait_ge(xs_lo_done, 4)
                            stream(n + r, ps[:, 2 + 3 * u + branch, 0:NT], xs_hi, xs_lo, 8 * branch, True, True
                                   ).then_inc(w_released, 1)
            pe.wait_ge(merged_lo, KT // 2)
            def out_tile(i, j):
                project(Place(OUT0 + 2 * j, (4, i)), Place(OUT_T + j, (2, i)), j, xs2_hi, xs2_lo)

            def pair_sums(p, i=None):
                pe.wait_ge(sq_done, p + 17 if i is None else i + (p + 17))
                for k in range(2):
                    last = pe.matmul(ps[:, 2, 0:NT], ones[:], sqh[:, k, :], start=i is None and p == 0 and k == 0,
                                     stop=p == KT // 2 - 1 and k == 1)
                last.then_inc(sq_summed, 1)

            for t in range(4):
                project(Place(OUT0 + 2 * t), Place(OUT_T + t), t % 2, xs2_hi, xs2_lo, second_half=(merged_lo, KT))
                if t == 2:
                    pair_sums(0)
            with pe.Fori(2, KT // 2) as i:
                out_tile(i, 0)
                pair_sums(-1, i)
                out_tile(i, 1)
            pair_sums(KT // 2 - 1)
            pe.wait_ge(xs_lo_done, 6)
            with pe.Fori(0, WQ_BLOCKS // 4) as i:
                for j in range(2):
                    project(Place(WQ0 + 2 * j, (4, i)), Place(WQ_T + j, (2, i)), j, xs_hi, xs_lo, second_half=(xs_lo_done, 8))
            with pe.Fori(0, PH // 2) as h2:
                for j in range(2 * SELECT_TILES):
                    project(Place(U0 + 2 * j, (4 * SELECT_TILES, h2)), Place(U_T + j, (2 * SELECT_TILES, h2)), j % 2,
                            xs_hi, xs_lo)
                    if j % SELECT_TILES == 1:
                        pe.wait_ge(t_staged, h2 * 2 + (j // SELECT_TILES + 1))
                        for t in range(3):
                            tok = min(t * P, NT - P)
                            for half, keys in enumerate((k1T, k2T)):
                                q = 2 * t + half
                                last = pe.matmul(ps[:, 2 + q // 3, (q % 3) * PK:(q % 3 + 1) * PK],
                                                 pq_st[:, half, tok:tok + P], keys, start=True, stop=True)
                        last.then_inc(t_scored, 1)
            project(Place(U0 + 2 * SPREAD_U), Place(U_T + SPREAD_U), 0, xs_hi, xs_lo)
            pe.wait_ge(r_done, PH)
            for t in range(3):
                for kind in range(3):
                    last = pe.transpose(ps[:, 2 + t, kind * P:(kind + 1) * P],
                                        R[:, t, kind, :, :].rearrange("p h k -> p (h k)"), ident[:])
            last.then_inc(r_turned, 1)
            pe.wait_ge(t_set, 1)
            with pe.Fori(0, NT // 64) as tb:
                for m in range(16):
                    pe.wait_ge(hot_set, tb * 16 + (m + 1))
                    pe.wait_ge(g_spread, tb * 16 + (m + 1))
                    for tk in range(4):
                        last = pe.matmul(ps[:, 2 + m % 2, tk * PK:(tk + 1) * PK], hot[:, m % 2, tk, 0, :],
                                         hot[:, m % 2, tk, 1, :], start=True, stop=True)
                    last.then_inc(hot_used, 1)
                    k = SPREAD_U + m + 1
                    project(Place(U0 + 2 * k, (32, tb)), Place(U_T + k, (16, tb)), k % 2, xs_hi, xs_lo)
            for k in range(LAST_U + 1, P):
                project(Place(U0 + 2 * k), Place(U_T + k), k % 2, xs_hi, xs_lo)
            with pe.Fori(0, 4) as gg:
                for group, (hi, lo) in enumerate(((xs2_hi, xs2_lo), (xs_hi, xs_lo))):
                    with pe.Fori(0, 8) as i:
                        pe.wait_ge(c_lo, gg * 16 + 8 * (group + 1))
                        for j in range(2):
                            project(Place(V0 + 32 * group + 2 * j, (4, i), (64, gg)),
                                    Place(V_T + 16 * group + j, (2, i), (32, gg)), j, hi, lo)


def _lay_out(inp):
    import numpy as np

    a = {}

    def c(x):
        return np.ascontiguousarray(x)

    def features(x):
        return c(x.T.reshape(-1, P, x.shape[0]).transpose(1, 0, 2))

    def vec(x):
        return x.reshape(-1, P).T

    def col_tiles(w):
        k, n = w.shape
        return c(w.reshape(k // (8 * P), 8, P, n // P, P).transpose(3, 0, 2, 1, 4).reshape(-1, P, BLK))

    x = np.concatenate([inp["x_prompt"].reshape(NP, D), inp["x_sample"].reshape(NB * NS, D)])
    a["xT"] = features(x)
    a["memT"] = features(inp["mem_prompt"][0])
    a["w_memk"] = col_tiles(inp["w_mem_k"][0])
    a["w_memv"] = c(inp["w_mem_v"][0].reshape(8, 2, P, 2, 512).transpose(3, 0, 2, 1, 4).reshape(-1, P, BLK))
    w_in = inp["w_in"][0]
    conv, gates0 = 2 * CC, w_in.shape[1] - 3 * D
    t = col_tiles(w_in[:, :gates0])
    ab = t[:2 * conv // P].reshape(2, CT, 2, P, BLK).transpose(1, 0, 2, 3, 4).reshape(-1, P, BLK)
    a["w_proj"] = c(np.concatenate([ab, t[2 * conv // P:]]))
    conv_o = inp["w_conv_o"][0].reshape(8, P, KT, P).transpose(2, 1, 0, 3).reshape(KT, P, BLK)
    mem_o = inp["w_mem_o"][0].reshape(8, P, KT, P).transpose(2, 1, 0, 3).reshape(KT, P, BLK)
    sw_o = inp["w_sw_o"][0].reshape(4, P, KT // 2, 2, P).transpose(2, 1, 3, 0, 4).reshape(KT // 2, P, BLK)
    oproj = np.stack([conv_o[0::2], mem_o[0::2], sw_o, conv_o[1::2], mem_o[1::2]], 1).reshape(-1, P, BLK)
    a["w_gate_oproj"] = c(np.concatenate([col_tiles(w_in[:, gates0:]), oproj]))
    a["w_out"] = col_tiles(inp["w_out"][0])
    a["w_q"] = col_tiles(inp["peer_w_q"][0])
    u = inp["peer_u"][0].reshape(P, P, 2, 8, P)
    a["w_u"] = c(u.transpose(1, 2, 4, 3, 0).reshape(-1, P, BLK))
    v = inp["peer_v"][0].reshape(P, 8, 2, 8, KT, P)
    a["w_v"] = c(v.transpose(1, 4, 2, 0, 3, 5).reshape(-1, P, BLK))
    a["params"] = c(np.concatenate([
        vec(inp["norm1_g"][0]), vec(inp["mem_norm_g"][0]), vec(inp["norm2_g"][0]),
        inp["conv_w"][0].reshape(CW, CT, P).transpose(2, 1, 0).reshape(P, -1),
        vec(inp["conv_b"][0]), vec(inp["conv_ln_g"][0]), vec(inp["conv_ln_b"][0]),
        inp["sw_q_g"][0].T, inp["sw_k_g"][0].T, vec(inp["mem_q_g"][0]), vec(inp["mem_k_g"][0]),
        inp["peer_k1"][0].T, inp["peer_k2"][0].T], axis=1))
    a["conv_state"] = c(inp["state_conv"][0].reshape(NB, CW - 1, CT, P).transpose(3, 2, 0, 1))
    k_units, v_units = [], []
    for g, (w, r) in enumerate(zip(WINDOWS, DILATIONS)):
        kk, vv = inp[f"state_sw{g}_k"][0], inp[f"state_sw{g}_v"][0]
        a[f"sw{g}_k"], a[f"sw{g}_v"] = c(kk.reshape(NB, -1)), c(vv.reshape(NB, -1))
        for cls in range(min(r, NS)):
            k_units.append(kk[:, cls::r].transpose(0, 3, 2, 1).reshape(NB, P, HG * P))
            v_units.append(vv[:, cls::r].reshape(NB, P, HG * P))
    a["k_units"], a["v_units"] = c(np.stack(k_units, 1)), c(np.stack(v_units, 1))
    ck, cv = inp["cache_mem_k"][0], inp["cache_mem_v"][0]
    a["memk_c"] = c(ck.reshape(NB, NM, MH, 2, P).transpose(0, 4, 2, 3, 1).reshape(NB, P, -1))
    a["memv_c"] = c(cv.reshape(NB, 2, P, MH * MD).transpose(0, 2, 1, 3).reshape(NB, P, -1))
    a["ident"] = np.eye(P, dtype=np.float32)
    a["iota"] = c(np.broadcast_to(np.arange(P, dtype=np.float32), (P, P)))
    a["iota16"] = c(np.broadcast_to(np.arange(TOPK, dtype=np.float32), (P, TOPK)))
    sl = np.array(slopes(), np.float32)
    a["slope"] = c(np.broadcast_to(-sl, (P, G * HG)))
    t, s = np.arange(NP)[:, None], np.arange(NP)[None, :]
    dist = np.stack([np.where((s <= t) & ((t - s) % r == 0) & (t - s <= P * r), t - s, 1e30) for r in DILATIONS], 1)
    a["dist_p"] = c(dist.reshape(2, P, G, NP).transpose(1, 0, 2, 3).astype(np.float32))
    bias = np.full((4, HG, NS, SAMPLE_COLS), NEG, np.float32)
    for g, (w, r) in enumerate(zip(WINDOWS, DILATIONS)):
        for h in range(HG):
            for q in range(NS):
                for m in range(P):
                    d = w + q - (q % r + r * m)
                    if d <= P * r:
                        bias[:, h, q, g * P + m] = -sl[g * HG + h] * d
                for q2 in range(q % r, q + 1, r):
                    for b in range(4):
                        bias[b, h, q, G * P + g * 32 + b * NS + q2] = -sl[g * HG + h] * (q - q2)
    a["dist_s"] = c(bias.reshape(P, SAMPLE_COLS))
    return a


def _outputs():
    o = {"y": (P, KT, NT), "convp": (P, CT, CW - 1), "convs": (P, CT, NB, CW - 1), "memk": (P, 2 * MH, NM),
         "memv": (2, P, MH * MD), "kp": (P, G * HG, NP), "vp": (P, 2, G * HG, P)}
    for g, w in enumerate(WINDOWS):
        o[f"sw{g}_k"] = o[f"sw{g}_v"] = (NB, w * HG * P)
    return o


def kernel(**inputs):
    import numpy as np
    import concourse.bacc as bacc
    from concourse.bass_utils import run_bass_kernel_spmd

    arrays = _lay_out({k: np.asarray(v) for k, v in inputs.items()})
    nc = bacc.Bacc("TRN2", target_bir_lowering=False, num_devices=1)
    a = {k: nc.dram_tensor("in_" + k, list(v.shape), F32, kind="ExternalInput").ap() for k, v in arrays.items()}
    o = {k: nc.dram_tensor("o_" + k, list(s), F32, kind="ExternalOutput").ap() for k, s in _outputs().items()}
    build(nc, a, o)
    r = run_bass_kernel_spmd(nc, [{"in_" + k: v for k, v in arrays.items()}], core_ids=[0]).results[0]
    r = {k: r["o_" + k] for k in o}

    y = r["y"].transpose(2, 1, 0).reshape(NT, D)
    kp = r["kp"].reshape(P, G, HG, NP).transpose(1, 3, 2, 0)
    vp = r["vp"].reshape(P, 2, G, HG, P).transpose(2, 1, 0, 3, 4).reshape(G, NP, HG, P)
    outs = [y[:NP].reshape(1, NP, D), y[NP:].reshape(NB, NS, D),
            r["convp"].transpose(2, 1, 0).reshape(1, 1, CW - 1, CC),
            r["convs"].transpose(2, 3, 1, 0).reshape(1, NB, CW - 1, CC)]
    for g, w in enumerate(WINDOWS):
        keep = min(w, NP)
        outs += [kp[g, NP - keep:].reshape(1, 1, keep, HG, P), vp[g, NP - keep:].reshape(1, 1, keep, HG, P)]
    for g, w in enumerate(WINDOWS):
        outs += [r[f"sw{g}_k"].reshape(1, NB, w, HG, P), r[f"sw{g}_v"].reshape(1, NB, w, HG, P)]
    outs += [r["memk"].reshape(P, MH, 2, NM).transpose(3, 1, 2, 0).reshape(1, 1, NM, MH, MD),
             r["memv"].reshape(1, 1, NM, MH, MD)]
    return tuple(np.ascontiguousarray(v) for v in outs)
```
